# Optimizing a Trainium2 kernel written in Bass

```python
import jax, jax.numpy as jnp
from jax import lax
import numpy as np

D_MODEL = 1024
BATCH = 1
SEQ = 512
DEPTH = 1

HEAD_DIM = 64
A_Q_HEADS = 8
A_KV_HEADS = 2
B_Q_HEADS = 8
B_KV_HEADS = 2
A_Q = A_Q_HEADS * HEAD_DIM
A_KV = A_KV_HEADS * HEAD_DIM
B_Q = B_Q_HEADS * HEAD_DIM
B_KV = B_KV_HEADS * HEAD_DIM
IN_COLS = A_Q + 2 * A_KV + B_Q + 2 * B_KV + 2 * D_MODEL
Q_BLOCK = 128
WINDOW = 128
GRID_W = 64
ROPE_THETA = 10000.0
N_EXPERTS = 32
TOP_K = 4
D_FF = 1024
SWIGLU_LIMIT = 7.0
SWIGLU_ALPHA = 1.702
MOE_BLOCK = 128
EPS = 1e-6
NEG_INF = -1e30

kernel_name = "hybrid_gated_gqa_window_sink_moe_encoder"

def rmsnorm(x, g):
    xf = x.astype(jnp.float32)
    y = xf * lax.rsqrt(jnp.mean(xf * xf, axis=-1, keepdims=True) + EPS)
    return (y * g.astype(jnp.float32)).astype(x.dtype)

def rope_rotate(x, cos, sin):
    half = x.shape[-1] // 2
    xf = x.astype(jnp.float32)
    x1, x2 = xf[..., :half], xf[..., half:]
    c = cos[:, None, :]
    s = sin[:, None, :]
    return jnp.concatenate([x1 * c - x2 * s, x2 * c + x1 * s], axis=-1).astype(x.dtype)

def rope_1d_tables(seq):
    pos = jnp.arange(seq, dtype=jnp.float32)
    inv = ROPE_THETA ** (-jnp.arange(0, HEAD_DIM, 2, dtype=jnp.float32) / HEAD_DIM)
    ang = pos[:, None] * inv[None, :]
    return jnp.cos(ang), jnp.sin(ang)

def rope_axial_tables(seq):
    rows = seq // GRID_W
    row = jnp.broadcast_to(jnp.arange(rows, dtype=jnp.float32)[:, None], (rows, GRID_W)).reshape(-1)
    col = jnp.broadcast_to(jnp.arange(GRID_W, dtype=jnp.float32)[None, :], (rows, GRID_W)).reshape(-1)
    axis_dim = HEAD_DIM // 2
    inv = ROPE_THETA ** (-jnp.arange(0, axis_dim, 2, dtype=jnp.float32) / axis_dim)
    ang = jnp.concatenate([row[:, None] * inv[None, :], col[:, None] * inv[None, :]], axis=-1)
    return jnp.cos(ang), jnp.sin(ang)

def global_axial_gqa(q, k, v, q_gain, k_gain, cos, sin):
    bsz, seq = q.shape[0], q.shape[1]
    q = rope_rotate(rmsnorm(q, q_gain), cos, sin)
    k = rope_rotate(rmsnorm(k, k_gain), cos, sin)
    groups = A_Q_HEADS // A_KV_HEADS
    nb = seq // Q_BLOCK
    scale = HEAD_DIM ** -0.5
    qb = q.reshape(bsz, nb, Q_BLOCK, A_KV_HEADS, groups, HEAD_DIM).transpose(1, 0, 2, 3, 4, 5)

    def one_block(qblk):
        s = jnp.einsum('bqkgd,bskd->bkgqs', qblk, k, preferred_element_type=jnp.float32) * scale
        p = jax.nn.softmax(s, axis=-1).astype(v.dtype)
        return jnp.einsum('bkgqs,bskd->bqkgd', p, v)

    o = lax.map(one_block, qb)
    return o.transpose(1, 0, 2, 3, 4, 5).reshape(bsz, seq, A_Q)

def window_sink_gqa(q, k, v, sink, cos, sin):
    bsz, seq = q.shape[0], q.shape[1]
    q = rope_rotate(q, cos, sin)
    k = rope_rotate(k, cos, sin)
    groups = B_Q_HEADS // B_KV_HEADS
    nb = seq // Q_BLOCK
    span = Q_BLOCK + 2 * WINDOW
    scale = HEAD_DIM ** -0.5
    qb = q.reshape(bsz, nb, Q_BLOCK, B_KV_HEADS, groups, HEAD_DIM)
    pad = ((0, 0), (WINDOW, WINDOW), (0, 0), (0, 0))
    kpad = jnp.pad(k, pad)
    vpad = jnp.pad(v, pad)
    kidx = jnp.arange(nb)[:, None] * Q_BLOCK + jnp.arange(span)[None, :]
    kwin = kpad[:, kidx]
    vwin = vpad[:, kidx]
    n = jnp.arange(nb)[:, None, None]
    qpos = n * Q_BLOCK + jnp.arange(Q_BLOCK)[None, :, None]
    kpos = n * Q_BLOCK - WINDOW + jnp.arange(span)[None, None, :]
    mask = (jnp.abs(kpos - qpos) <= WINDOW) & (kpos >= 0) & (kpos < seq)
    s = jnp.einsum('bnqkgd,bnjkd->bnkgqj', qb, kwin, preferred_element_type=jnp.float32) * scale
    s = jnp.where(mask[None, :, None, None], s, NEG_INF)
    sink_logit = jnp.broadcast_to(
        sink.astype(jnp.float32).reshape(1, 1, B_KV_HEADS, groups, 1, 1), s.shape[:-1] + (1,))
    p = jax.nn.softmax(jnp.concatenate([s, sink_logit], axis=-1), axis=-1)[..., :-1]
    o = jnp.einsum('bnkgqj,bnjkd->bnqkgd', p.astype(v.dtype), vwin)
    return o.reshape(bsz, seq, B_Q)

def clamped_swiglu(gu):
    gate, up = gu[..., :D_FF], gu[..., D_FF:]
    gate = jnp.minimum(gate, SWIGLU_LIMIT)
    up = jnp.clip(up, -SWIGLU_LIMIT, SWIGLU_LIMIT)
    return (up + 1.0) * (gate * jax.nn.sigmoid(SWIGLU_ALPHA * gate))

def moe(h, w_router, b_router, w_gate_up, b_gate_up, w_down, b_down):
    bsz, seq, d = h.shape
    T = bsz * seq
    hf = h.reshape(T, d)
    logits = jnp.einsum('td,de->te', hf, w_router, preferred_element_type=jnp.float32) \
        + b_router.astype(jnp.float32)
    top_vals, top_idx = lax.top_k(logits, TOP_K)
    gate = jax.nn.softmax(top_vals, axis=-1)
    A = T * TOP_K
    e_flat = top_idx.reshape(A)
    tok_flat = jnp.arange(A, dtype=jnp.int32) // TOP_K
    g_flat = gate.reshape(A)
    order = jnp.argsort(e_flat, stable=True)
    e_sorted = e_flat[order]
    counts = jnp.bincount(e_flat, length=N_EXPERTS)
    padded = (counts + MOE_BLOCK - 1) // MOE_BLOCK * MOE_BLOCK
    ends_p = jnp.cumsum(padded)
    starts_p = ends_p - padded
    starts = jnp.cumsum(counts) - counts
    rank = jnp.arange(A, dtype=jnp.int32) - starts[e_sorted]
    dest = starts_p[e_sorted] + rank
    n_blocks = -(-A // MOE_BLOCK) + N_EXPERTS
    R = n_blocks * MOE_BLOCK
    row_tok = jnp.full((R,), T, jnp.int32).at[dest].set(tok_flat[order])
    row_gate = jnp.zeros((R,), jnp.float32).at[dest].set(g_flat[order])
    block_exp = jnp.minimum(
        jnp.searchsorted(ends_p, jnp.arange(n_blocks) * MOE_BLOCK, side='right'), N_EXPERTS - 1)
    h_pad = jnp.concatenate([hf, jnp.zeros((1, d), hf.dtype)], axis=0)
    xs = h_pad[row_tok].reshape(n_blocks, MOE_BLOCK, d)

    def run_block(args):
        xb, e = args
        gu = xb @ w_gate_up[e] + b_gate_up[e]
        return clamped_swiglu(gu) @ w_down[e] + b_down[e]

    ys = lax.map(run_block, (xs, block_exp)).reshape(R, d)
    ys = ys.astype(jnp.float32) * row_gate[:, None]
    out = jax.ops.segment_sum(ys, row_tok, num_segments=T + 1)[:T]
    return out.astype(h.dtype).reshape(bsz, seq, d)

def setup_inputs(seed: int = 0) -> dict:
    key = jax.random.key(seed)
    ks = jax.random.split(key, 20)
    f32 = jnp.float32
    nrm = lambda k, shape: jax.random.normal(k, shape, dtype=f32)
    L, D, E, F = DEPTH, D_MODEL, N_EXPERTS, D_FF
    return {
        "x": nrm(ks[0], (BATCH, SEQ, D)),
        "g_mix": 1.0 + 0.02 * nrm(ks[1], (L, D)),
        "w_in": nrm(ks[2], (L, D, IN_COLS)) * D ** -0.5,
        "qa_norm": 1.0 + 0.02 * nrm(ks[3], (L, HEAD_DIM)),
        "ka_norm": 1.0 + 0.02 * nrm(ks[4], (L, HEAD_DIM)),
        "sink_b": 0.5 * nrm(ks[5], (L, B_Q_HEADS)),
        "w_branch_a": nrm(ks[6], (L, A_Q, D)) * A_Q ** -0.5,
        "w_branch_b": nrm(ks[7], (L, B_Q, D)) * B_Q ** -0.5,
        "w_out": nrm(ks[8], (L, D, D)) * D ** -0.5,
        "g_ffn": 1.0 + 0.02 * nrm(ks[9], (L, D)),
        "w_router": nrm(ks[10], (L, D, E)) * D ** -0.5,
        "b_router": 0.01 * nrm(ks[11], (L, E)),
        "w_gate_up": nrm(ks[12], (L, E, D, 2 * F)) * D ** -0.5,
        "b_gate_up": 0.01 * nrm(ks[13], (L, E, 2 * F)),
        "w_down": nrm(ks[14], (L, E, F, D)) * F ** -0.5,
        "b_down": 0.01 * nrm(ks[15], (L, E, D)),
        "g_final": 1.0 + 0.02 * nrm(ks[16], (D,)),
    }

def reference(x, g_mix, w_in, qa_norm, ka_norm, sink_b, w_branch_a, w_branch_b, w_out,
              g_ffn, w_router, b_router, w_gate_up, b_gate_up, w_down, b_down, g_final):
    bsz, seq, _ = x.shape
    cos_ax, sin_ax = rope_axial_tables(seq)
    cos_1d, sin_1d = rope_1d_tables(seq)
    splits = np.cumsum([A_Q, A_KV, A_KV, B_Q, B_KV, B_KV, D_MODEL]).tolist()
    for l in range(DEPTH):
        h = rmsnorm(x, g_mix[l])
        proj = h @ w_in[l]
        qa, ka, va, qb, kb, vb, gate_a, gate_b = jnp.split(proj, splits, axis=-1)
        qa = qa.reshape(bsz, seq, A_Q_HEADS, HEAD_DIM)
        ka = ka.reshape(bsz, seq, A_KV_HEADS, HEAD_DIM)
        va = va.reshape(bsz, seq, A_KV_HEADS, HEAD_DIM)
        qb = qb.reshape(bsz, seq, B_Q_HEADS, HEAD_DIM)
        kb = kb.reshape(bsz, seq, B_KV_HEADS, HEAD_DIM)
        vb = vb.reshape(bsz, seq, B_KV_HEADS, HEAD_DIM)
        oa = global_axial_gqa(qa, ka, va, qa_norm[l], ka_norm[l], cos_ax, sin_ax)
        ob = window_sink_gqa(qb, kb, vb, sink_b[l], cos_1d, sin_1d)
        merged = jax.nn.sigmoid(gate_a) * (oa @ w_branch_a[l]) \
            + jax.nn.sigmoid(gate_b) * (ob @ w_branch_b[l])
        x = x + merged @ w_out[l]
        h2 = rmsnorm(x, g_ffn[l])
        x = x + moe(h2, w_router[l], b_router[l], w_gate_up[l], b_gate_up[l], w_down[l], b_down[l])
    return rmsnorm(x, g_final)


_drawn_inputs = setup_inputs


def setup_inputs(seed=0):
    import zlib

    import numpy as np

    out = dict(_drawn_inputs(seed))
    spreads = {}
    factors = {'g_mix': 3.598,
     'qa_norm': 6.707,
     'ka_norm': 8.0,
     'sink_b': 64.0,
     'b_gate_up': 28.463,
     'b_down': 33.095,
     'g_final': 8.153,
     'g_ffn': 3.299,
     'b_router': 4.682}
    for name, (base, spread) in spreads.items():
        noise = np.random.default_rng([zlib.crc32(name.encode()), seed]).standard_normal(out[name].shape)
        drawn = base * np.exp(spread * noise) if base else spread * noise
        out[name] = __import__('jax').numpy.asarray(drawn.astype(out[name].dtype))
    for name, factor in factors.items():
        out[name] = (out[name] * factor).astype(out[name].dtype)
    return out
```

```python
import numpy as np
import concourse.bass as bass
from concourse import mybir
from contextlib import ExitStack

SEQ, D, HD = 512, 1024, 64
NT, KD = SEQ // 128, D // 128
E, FF, TOPK = 32, 1024, 4
CAP = 96
PASSES = -(-SEQ // CAP)
EPS = 1e-6
SLOT = 2048
NSLOT, NRING = 12, 8


def encoder_block(nc, x, g_mix, w_in, qa_norm, ka_norm, sink_b, w_branch_a, w_branch_b, w_out, g_ffn, w_router,
                  b_router, w_gate_up, b_gate_up, w_down, b_down, g_final, rope, h2buf, acc, out):
    F32, BF16, I32 = mybir.dt.float32, mybir.dt.bfloat16, mybir.dt.int32
    ALU, ACT, AX = mybir.AluOpType, mybir.ActivationFunctionType, mybir.AxisListType
    NEG = -1e30
    ROWS = SEQ + CAP
    JOBS = 16
    SCALE = HD ** -0.5

    ctx = ExitStack()
    with ctx:
        def sb(name, shape, dt=F32):
            return ctx.enter_context(nc.sbuf_tensor(name, shape, dt))

        def sem(name):
            return ctx.enter_context(nc.semaphore(name))

        ring = sb("ring", [128, NSLOT, SLOT])
        xs = sb("xs", [128, NT, D])
        reg_h = sb("reg_h", [128, 4096])
        reg_q = sb("reg_q", [128, 6144])
        reg_k = sb("reg_k", [128, 6144])
        reg_r = sb("reg_r", [128, 3584])

        gT = ring[:, NRING:NSLOT, :].rearrange("p s (t n) -> p (s t) n", n=SEQ)
        zeros = ring[0:CAP, NRING, 0:D]
        hT = reg_h[:, :].rearrange("p (k n) -> p k n", n=SEQ)
        oT = hT
        bias32 = reg_h[:, 0:3 * D]
        gfin = reg_h[:, 3 * D:4 * D]
        qT = reg_q[:, :].rearrange("p (t n) -> p t n", n=SEQ)
        mT = reg_q[:, 0:KD * SEQ].rearrange("p (t n) -> p t n", n=SEQ)
        xn = reg_k[:, 0:NT * D].rearrange("p (c n) -> p c n", n=D)
        qk = reg_k[:, :].rearrange("p (c n) -> p c n", n=1536)
        probs = reg_k[:, 0:4096].rearrange("p (b n w) -> p b n w", b=2, w=512)
        rt1 = reg_r[:, 0:768]
        rt2 = reg_r[:, 768:1536]
        pT = reg_r[:, 0:2048].rearrange("p (k n) -> p k n", n=SEQ)
        v_sb = reg_r[:, 2048:3072].rearrange("p (c n) -> p c n", n=256)
        mtmp = reg_r[:, 0:1024].rearrange("p (b n) -> p b n", b=2)
        h2T = reg_r[:, 0:2048].rearrange("p (b k n) -> p b k n", b=2, n=128)
        bias_tab = reg_r[:, 2048:3584].bitcast(BF16)
        xg = reg_q[0:CAP, 0:1024]
        hid = reg_q[0:CAP, 1024:2048]
        ysb = reg_q[0:CAP, 2048:3072]
        gc = reg_q[0:CAP, 3072:3584]
        uc = reg_q[0:CAP, 3584:4096]
        sg = reg_q[0:CAP, 4096:4608]
        XT = reg_q[:, 4608:4608 + KD * CAP].rearrange("p (k n) -> p k n", n=CAP)
        hidT = reg_q[:, 5376:5376 + KD * CAP].rearrange("p (k n) -> p k n", n=CAP)

        ident = sb("ident", [128, 128])
        identb = sb("identb", [128, 128], BF16)
        mask_lo = sb("mask_lo", [128, 128], BF16)
        mask_hi = sb("mask_hi", [128, 128], BF16)
        mask_all = sb("mask_all", [128, 128], BF16)
        tri = sb("tri", [128, 128], BF16)
        onesb = sb("onesb", [128, 128], BF16)
        iota_cap = sb("iota_cap", [128, CAP])
        part_mod = sb("part_mod", [128, CAP])
        erow = sb("erow", [128, E])
        passoff = sb("passoff", [128, 8])
        idle_row = sb("idle_row", [128, 1])
        idle_neg = sb("idle_neg", [128, 1])
        feats = sb("feats", [128, NT, E, 6], BF16)
        rp = sb("rp", [128, NT, 4, 32])
        gains = sb("gains", [128, 2, HD])
        sink = sb("sink", [128, 8])
        brt = sb("brt", [128, E])
        wr = sb("wr", [128, KD, E])
        g16 = sb("g16", [16, 128])
        g4 = sb("g4", [4, 256])
        gcol = sb("gcol", [128, 24])
        eps = sb("eps", [128, 1])
        ss = sb("ss", [128, NT])
        rstd = sb("rstd", [128, NT])
        hs = sb("hs", [128, NT, 12])
        diag = sb("diag", [128, 4, 128])
        mx = sb("mx", [128, 4])
        negm = sb("negm", [128, 2, 4])
        esink = sb("esink", [128, 2, 4])
        psum_p = sb("psum_p", [128, 2, 4])
        rinv = sb("rinv", [128, 4])
        lg = sb("lg", [128, NT, E])
        m8 = sb("m8", [128, 8])
        m8x = sb("m8x", [128, 8])
        repl = sb("repl", [128, E])
        mask = sb("mask", [128, NT, E], BF16)
        negl = sb("negl", [128, NT])
        ex = sb("ex", [128, NT, E])
        gsum = sb("gsum", [128, 1])
        posx = sb("posx", [128, NT, E])
        cmax = sb("cmax", [128, 1])
        over = sb("over", [128, 8])
        npass = sb("npass", [128, 1])
        items_i = sb("items_i", [128, 1], I32)
        tgt = sb("tgt", [128, NT])
        onehot = sb("onehot", [128, NT, CAP], BF16)
        sel = sb("sel", [128, CAP], BF16)
        f6 = sb("f6", [CAP, 6])
        s1 = sb("s1", [CAP, 1])
        s2 = sb("s2", [CAP, 1])
        idx_g = sb("idx_g", [CAP, 1], I32)
        idx_s = sb("idx_s", [CAP, 1], I32)
        gate_c = sb("gate_c", [CAP, 1])

        ps = ctx.enter_context(nc.psum_tensor("ps", [128, 8, 512], F32))
        idx_ps = ps[0:CAP, 7, 448:454]

        x_in = [sem(f"x_in{c}") for c in range(NT)]
        consts_in = sem("consts_in")
        slot_full = [sem(f"slot_full{s}") for s in range(NSLOT)]
        chunks_used = sem("chunks_used")
        item_chunks_used = sem("item_chunks_used")
        pool_step = sem("pool_step")
        pool_past = sem("pool_past")
        zero_set = sem("zero_set")
        pool_consts = sem("pool_consts")
        part_mod_set = sem("part_mod_set")
        zeros_stored = sem("zeros_stored")
        gcol_ps = sem("gcol_ps")
        gcol_ready = sem("gcol_ready")
        sq_done = sem("sq_done")
        rt_done = sem("rt_done")
        dve_step = sem("dve_step")
        xn_ready = sem("xn_ready")
        hT_ps = sem("hT_ps")
        hT_a = sem("hT_a")
        hT_d = sem("hT_d")
        proj_ps = sem("proj_ps")
        proj_out = sem("proj_out")
        hs_ready = sem("hs_ready")
        hrt_done = sem("hrt_done")
        rope_done = sem("rope_done")
        qT_ps = sem("qT_ps")
        qT_a = sem("qT_a")
        qT_d = sem("qT_d")
        scores_ps = sem("scores_ps")
        negm_ready = sem("negm_ready")
        exps_done = sem("exps_done")
        esink_done = sem("esink_done")
        diag_ready = sem("diag_ready")
        pT_ps = sem("pT_ps")
        pT_a = sem("pT_a")
        pT_d = sem("pT_d")
        pv_ps = sem("pv_ps")
        oT_out = sem("oT_out")
        branch_ps = sem("branch_ps")
        merged = sem("merged")
        wout_ps = sem("wout_ps")
        x1_ready = sem("x1_ready")
        sq2_done = sem("sq2_done")
        rt2_done = sem("rt2_done")
        rstd2_ready = sem("rstd2_ready")
        xn2_ready = sem("xn2_ready")
        rows_stored = sem("rows_stored")
        h2T_ps = sem("h2T_ps")
        h2T_out = sem("h2T_out")
        logits_ps = sem("logits_ps")
        lg_ready = sem("lg_ready")
        ex_done = sem("ex_done")
        mask_ready = sem("mask_ready")
        pos_ps = sem("pos_ps")
        route_ready = sem("route_ready")
        items_ready = sem("items_ready")
        bias_in = sem("bias_in")
        bias_ready = sem("bias_ready")
        onehot_ready = sem("onehot_ready")
        idx_done = sem("idx_done")
        idx_ready = sem("idx_ready")
        idx_kept = sem("idx_kept")
        gathered = sem("gathered")
        scattered = sem("scattered")
        xt_ps = sem("xt_ps")
        xt_ready = sem("xt_ready")
        sel_ready = sem("sel_ready")
        gate_ready = sem("gate_ready")
        pair_ps = sem("pair_ps")
        clamp_ready = sem("clamp_ready")
        sig_done = sem("sig_done")
        hid_ready = sem("hid_ready")
        hidT_ps = sem("hidT_ps")
        hidT_ready = sem("hidT_ready")
        down_begun = sem("down_begun")
        y_ps = sem("y_ps")
        y_ready = sem("y_ready")
        acc_in = [sem(f"acc_in{c}") for c in range(NT)]
        gfin_in = sem("gfin_in")
        fsq_done = sem("fsq_done")
        frt_done = sem("frt_done")
        out_ready = sem("out_ready")
        out_stored = sem("out_stored")

        def kp(ap):
            return ap.rearrange("(k p) n -> p k n", p=128)

        chunk_src = []
        for g in range(7):
            for s in range(2):
                chunk_src.append(kp(w_in[0, s * 512:(s + 1) * 512, g * 512:(g + 1) * 512]))
        for w in (w_branch_a, w_branch_b, w_out):
            for s in range(w.shape[1] // 256):
                chunk_src.append(kp(w[0, s * 256:(s + 1) * 256, :]))
        BR_A, BR_B, W_OUT, CHUNKS = 14, 16, 18, 22
        loads_before = [len(range(s, CHUNKS, NRING)) if s < NRING else 0 for s in range(NSLOT)]

        def chunk(n, width):
            return ring[:, n % NRING, :].rearrange("p (k n) -> p k n", n=width)

        def wait_chunk(eng, n):
            eng.wait_ge(slot_full[n % NRING], 16 * (n // NRING + 1))

        def expert_src(e, s):
            if s < 8:
                half, k2 = s // 4, s % 4
                w = w_gate_up[0, e, k2 * 256:(k2 + 1) * 256, :].rearrange("(p k) (t n) -> p (k t) n", k=2, t=2)
                return w[:, :, half * 512:(half + 1) * 512]
            return w_down[0, e, (s - 8) * 256:(s - 7) * 256, :].rearrange("(k p) n -> p k n", p=128)

        def expert_dst(s):
            if s < 8:
                return ring[:, s, :].rearrange("p (a n) -> p a n", a=4)
            return ring[:, s, :].rearrange("p (k n) -> p k n", k=2)

        def expert_w(s, k, t):
            return ring[:, s, (2 * k + t) * 512:(2 * k + t + 1) * 512]

        def window(n):
            return [kb for kb in (n - 1, n, n + 1) if 0 <= kb < NT]

        WW = 384

        block = ctx.enter_context(nc.Block())

        @block.sync
        def _(sp):
            x_v = x.rearrange("b (c p) n -> (b c) p n", p=128)
            for c in range(NT):
                sp.dma_start(xs[:, c, :], x_v[c]).then_inc(x_in[c], 16)
            for n in range(CHUNKS):
                if n >= NRING:
                    sp.wait_ge(chunks_used, n - NRING + 1)
                w = chunk_src[n]
                sp.dma_start(chunk(n, w.shape[2]), w).then_inc(slot_full[n % NRING], 16)
            for s in (6, 7, 0, 1, 8, 9, 10, 11, 2, 3, 4, 5):
                if s in (6, 7, 0, 1):
                    sp.wait_ge(chunks_used, W_OUT)
                elif s >= NRING:
                    sp.wait_ge(merged, KD)
                else:
                    sp.wait_ge(chunks_used, CHUNKS)
                sp.dma_start(expert_dst(s), expert_src(0, s)).then_inc(slot_full[s], 16)
            sp.wait_ge(items_ready, 1)
            items = sp.value_load(items_i[0:1, 0:1], min_val=E, max_val=E * PASSES)
            with sp.Fori(1, items) as i:
                for s in range(NSLOT):
                    sp.wait_ge(item_chunks_used, (i - 1) * NSLOT + s + 1)
                    sp.dma_start(expert_dst(s), expert_src(i % E, s)).then_inc(slot_full[s], 16)
            sp.wait_ge(scattered, items * 16)
            acc_v = acc[0:SEQ, :].rearrange("(c p) n -> c p n", p=128)
            out_v = out.rearrange("b (c p) n -> (b c) p n", p=128)
            for c in range(NT):
                sp.dma_start(xs[:, c, :], acc_v[c]).then_inc(acc_in[c], 16)
            for c in range(NT):
                sp.wait_ge(out_ready, c + 1)
                sp.dma_start(out_v[c], xs[:, c, :]).then_inc(out_stored, 16)
            sp.wait_ge(out_stored, 16 * NT)

        @block.gpsimd
        def _(pool):
            g = nc.gpsimd
            g.memset(zeros, 0.0).then_inc(zero_set, 1)
            g.memset(ident[:, :], 0.0)
            g.memset(identb[:, :], 0.0)
            g.memset(mask_lo[:, :], 0.0)
            g.memset(mask_hi[:, :], 0.0)
            g.memset(mask_all[:, :], NEG)
            g.memset(tri[:, :], 1.0)
            g.memset(onesb[:, :], 1.0)
            g.memset(part_mod[:, :], 999.0)
            g.memset(eps[:, :], EPS)
            g.memset(feats[:, :, :, 2:3], 1.0).then_inc(pool_step, 1)
            pool.wait_ge(pool_step, 1)
            for t in (ident, identb):
                g.affine_select(out=t[:, :], in_=t[:, :], compare_op=ALU.not_equal, fill=1.0, base=0,
                                pattern=[[-1, 128]], channel_multiplier=1)
            g.affine_select(out=mask_lo[:, :], in_=mask_lo[:, :], compare_op=ALU.is_ge, fill=NEG, base=0,
                            pattern=[[1, 128]], channel_multiplier=-1)
            g.affine_select(out=mask_hi[:, :], in_=mask_hi[:, :], compare_op=ALU.is_ge, fill=NEG, base=0,
                            pattern=[[-1, 128]], channel_multiplier=1)
            g.affine_select(out=tri[:, :], in_=tri[:, :], compare_op=ALU.is_ge, fill=0.0, base=-1,
                            pattern=[[1, 128]], channel_multiplier=-1)
            g.iota(iota_cap[:, :], pattern=[[1, CAP]], base=0, channel_multiplier=0,
                   allow_small_or_imprecise_dtypes=True)
            g.iota(erow[:, :], pattern=[[1, E]], base=0, channel_multiplier=0, allow_small_or_imprecise_dtypes=True)
            g.iota(passoff[:, :], pattern=[[CAP, 8]], base=0, channel_multiplier=0,
                   allow_small_or_imprecise_dtypes=True)
            g.iota(idle_row[:, :], pattern=[[0, 1]], base=SEQ, channel_multiplier=1,
                   allow_small_or_imprecise_dtypes=True)
            g.iota(idle_neg[:, :], pattern=[[0, 1]], base=-SEQ, channel_multiplier=-1,
                   allow_small_or_imprecise_dtypes=True)
            g.iota(feats[:, :, :, 0:1], pattern=[[0, NT], [0, E], [0, 1]], base=0, channel_multiplier=1,
                   allow_small_or_imprecise_dtypes=True)
            g.iota(feats[:, :, :, 1:2], pattern=[[128, NT], [0, E], [0, 1]], base=0, channel_multiplier=0,
                   allow_small_or_imprecise_dtypes=True).then_inc(pool_consts, 1)
            pool.wait_ge(pool_consts, 1)
            for q in range(3):
                g.iota(part_mod[32 * q:32 * q + 32, :], pattern=[[0, CAP]], base=0, channel_multiplier=1,
                       allow_small_or_imprecise_dtypes=True).then_inc(part_mod_set, 1)
                pool.wait_ge(part_mod_set, q + 1)
            pool.wait_ge(zero_set, 1)
            pool.dma_start(h2buf[SEQ:ROWS, :], zeros).then_inc(zeros_stored, 16)
            pool.dma_start(acc[SEQ:ROWS, :], zeros).then_inc(zeros_stored, 16)

            pool.wait_ge(chunks_used, W_OUT)
            for q in range(3):
                rows = slice(32 * q, 32 * q + 32)
                pool.dma_start(bias32[rows, 0:2 * FF], b_gate_up[0]).then_inc(bias_in, 16)
                pool.dma_start(bias32[rows, 2 * FF:3 * FF], b_down[0]).then_inc(bias_in, 16)
            pool.wait_ge(bias_in, 96)
            chain = [1]

            def link(ins):
                chain[0] += 1
                ins.then_inc(pool_step, 1)
                pool.wait_ge(pool_step, chain[0])

            part1, part2 = slice(32, 64), slice(64, 96)
            link(g.memset(bias_tab[96:128, :], 0.0))
            link(g.tensor_copy(bias_tab[0:96, :], bias32[0:96, :]))
            for rows in (part1, part2):
                link(g.tensor_tensor(bias32[rows, :], bias32[rows, :], bias_tab[rows, :], ALU.subtract))
                link(g.tensor_copy(bias_tab[rows, :], bias32[rows, :]))
            link(g.tensor_tensor(bias32[part2, :], bias32[part2, :], bias_tab[part2, :], ALU.subtract))
            g.tensor_copy(bias_tab[part2, :], bias32[part2, :]).then_inc(bias_ready, 1)
            pool.wait_ge(bias_ready, 1)

            pool.wait_ge(rows_stored, 2 * NT * 16)
            pool.wait_ge(zeros_stored, 32)
            pool.wait_ge(items_ready, 1)
            items = pool.value_load(items_i[0:1, 0:1], min_val=E, max_val=E * PASSES)

            def gather():
                g.indirect_dma_start(out=xg, out_offset=None, in_=h2buf,
                                     in_offset=bass.IndirectOffsetOnAxis(ap=idx_g[:, 0:1], axis=0)
                                     ).then_inc(gathered, 16)

            pool.wait_ge(idx_ready, 1)
            gather()
            g.tensor_copy(idx_s[:, :], idx_g[:, :]).then_inc(idx_kept, 1)
            with pool.Fori(0, items) as i:
                pool.wait_ge(idx_ready, i + 2)
                pool.wait_ge(xt_ps, i + 1)
                pool.sem_inc(pool_past, 1)
                gather()
                pool.wait_ge(y_ready, 2 * i + 3)
                pool.wait_ge(idx_kept, i + 1)
                pool.sem_inc(pool_past, 1)
                g.indirect_dma_start(out=acc, out_offset=bass.IndirectOffsetOnAxis(ap=idx_s[:, 0:1], axis=0),
                                     in_=ysb, in_offset=None, compute_op=ALU.add).then_inc(scattered, 16)
                pool.wait_ge(scattered, 16 * i + 16)
                pool.sem_inc(pool_past, 1)
                g.tensor_copy(idx_s[:, :], idx_g[:, :]).then_inc(idx_kept, 1)

        @block.scalar
        def _(act):
            a = nc.scalar
            act.dma_start(g16[0:8, :], g_mix.rearrange("l (k p) -> (l k) p", p=128)).then_inc(consts_in, 16)
            act.dma_start(g16[8:16, :], g_ffn.rearrange("l (k p) -> (l k) p", p=128)).then_inc(consts_in, 16)
            act.dma_start(g4[:, :], g_ffn.rearrange("l (k p) -> (l k) p", p=256)).then_inc(consts_in, 16)
            act.dma_start(rp[:, :, :, :], rope.rearrange("(c p) t n -> p c t n", p=128)).then_inc(consts_in, 16)
            act.dma_start(gains[:, 0, :], qa_norm[0:1, :].to_broadcast([128, HD])).then_inc(consts_in, 16)
            act.dma_start(gains[:, 1, :], ka_norm[0:1, :].to_broadcast([128, HD])).then_inc(consts_in, 16)
            act.dma_start(sink[:, :], sink_b[0:1, :].to_broadcast([128, 8])).then_inc(consts_in, 16)
            act.dma_start(brt[:, :], b_router[0:1, :].to_broadcast([128, E])).then_inc(consts_in, 16)
            act.dma_start(wr[:, :, :], kp(w_router[0])).then_inc(consts_in, 16)
            act.wait_ge(pool_consts, 1)
            for c in range(NT):
                act.wait_ge(x_in[c], 16)
                a.activation(xn[:, c, :], xs[:, c, :], ACT.Square, accum_out=ss[:, c:c + 1]).then_inc(sq_done, 1)
                act.wait_ge(sq_done, c + 1)
                a.activation(ss[:, c:c + 1], ss[:, c:c + 1], ACT.Sqrt, bias=eps[:, 0:1],
                             scale=1.0 / D).then_inc(rt_done, 1)
            act.wait_ge(gcol_ready, 1)
            for k in range(0, KD, 2):
                act.wait_ge(hT_ps, k + 1)
                a.activation(hT[:, k, :], ps[:, k, :], ACT.Copy, scale=gcol[:, k:k + 1]).then_inc(hT_a, 1)
            act.wait_ge(xn_ready, NT)
            for n in range(12):
                grp, c = n // NT, n % NT
                act.wait_ge(proj_ps, n + 1)
                src = ps[:, n % 4, :]
                if grp == 0:
                    a.activation(qk[:, c, 0:512], src, ACT.Copy).then_inc(proj_out, 1)
                    continue
                if grp == 1:
                    kv, q, q_at, k_at, v_at = src[:, 0:256], src[:, 256:512], 768, 512, 0
                else:
                    kv, q, q_at, k_at, v_at = src[:, 256:512], src[:, 0:256], 1024, 1280, 128
                a.activation(qk[:, c, q_at:q_at + 256], q, ACT.Copy)
                k_dst = qk[:, c, k_at:k_at + 256].rearrange("p (h two n) -> p h two n", h=2, two=2)
                k_src = kv[:, 0:128].rearrange("p (h n) -> p h n", h=2)
                a.activation(k_dst[:, :, 0, :], k_src, ACT.Copy)
                a.activation(k_dst[:, :, 1, :], k_src, ACT.Copy)
                a.activation(v_sb[:, c, v_at:v_at + 128], kv[:, 128:256], ACT.Copy).then_inc(proj_out, 1)
            act.wait_ge(zeros_stored, 32)
            for n in range(12, 28):
                act.wait_ge(proj_ps, n + 1)
                a.activation(gT[:, n - 12, :], ps[:, n % 4, :], ACT.Sigmoid).then_inc(proj_out, 1)
                if n % 4 == 3:
                    c = (n - 15) // 4
                    act.wait_ge(hs_ready, c + 1)
                    a.activation(hs[:, c, :], hs[:, c, :], ACT.Sqrt, bias=eps[:, 0:1],
                                 scale=1.0 / HD).then_inc(hrt_done, 1)
            for n in range(1, 12, 2):
                act.wait_ge(qT_ps, n + 1)
                c, t = n // 3, n % 3
                a.activation(qT[:, 4 * t:4 * t + 4, c * 128:(c + 1) * 128],
                             ps[:, 4 + t, :].rearrange("p (t n) -> p t n", n=128), ACT.Copy).then_inc(qT_a, 1)

            def exps(j):
                w = SEQ if j < 8 else WW
                act.wait_ge(negm_ready, j + 1)
                if j >= 2:
                    act.wait_ge(pT_ps, 4 * (j - 1))
                for n in range(4):
                    a.activation(probs[:, j % 2, n, 0:w], ps[:, n, 0:w], ACT.Exp, bias=negm[:, j % 2, n:n + 1],
                                 scale=SCALE, accum_out=psum_p[:, j % 2, n:n + 1]).then_inc(exps_done, 1)
                if j >= 8:
                    a.activation(esink[:, j % 2, :], negm[:, j % 2, :], ACT.Exp,
                                 bias=sink[:, j - 8:j - 7]).then_inc(esink_done, 1)

            exps(0)
            for j in range(JOBS):
                for kb in range(2):
                    act.wait_ge(pT_ps, 4 * j + kb + 1)
                    if j:
                        act.wait_ge(pv_ps, j)
                    q0, q1 = (0, NT) if j < 8 else (window(kb)[0], window(kb)[-1] + 1)
                    a.activation(pT[:, kb, q0 * 128:q1 * 128], ps[:, 4 + (4 * j + kb) % 3, q0 * 128:q1 * 128],
                                 ACT.Copy).then_inc(pT_a, 1)
                if j + 1 < JOBS:
                    exps(j + 1)

            def choice_exp(c):
                act.wait_ge(lg_ready, c + 1)
                a.activation(ex[:, c, :], lg[:, c, :], ACT.Exp, bias=negl[:, c:c + 1]).then_inc(ex_done, 1)

            act_v = acc[0:SEQ, :].rearrange("(c p) n -> c p n", p=128)
            h2_v = h2buf[0:SEQ, :].rearrange("(c p) n -> c p n", p=128)
            for c in range(NT):
                act.wait_ge(x1_ready, 2 * c + 2)
                act.dma_start(act_v[c], xs[:, c, :]).then_inc(rows_stored, 16)
                a.activation(xn[:, c, :], xs[:, c, :], ACT.Square, accum_out=ss[:, c:c + 1]).then_inc(sq2_done, 1)
                act.wait_ge(sq2_done, c + 1)
                a.activation(ss[:, c:c + 1], ss[:, c:c + 1], ACT.Sqrt, bias=eps[:, 0:1],
                             scale=1.0 / D).then_inc(rt2_done, 1)
                act.wait_ge(rstd2_ready, c + 1)
                a.activation(xn[:, c, :], xs[:, c, :], ACT.Copy, scale=rstd[:, c:c + 1]).then_inc(xn2_ready, 1)
                act.wait_ge(xn2_ready, c + 1)
                act.dma_start(h2_v[c], xn[:, c, :]).then_inc(rows_stored, 16)
                if c >= 2:
                    choice_exp(c - 2)
            choice_exp(2)
            choice_exp(3)

            act.wait_ge(items_ready, 1)
            items = act.value_load(items_i[0:1, 0:1], min_val=E, max_val=E * PASSES)
            act.sem_inc(hidT_ready, 1)
            act.sem_inc(y_ready, 1)
            with act.Fori(0, items) as i:
                for half in range(2):
                    act.wait_ge(clamp_ready, 2 * i + half + 1)
                    a.activation(sg, gc, ACT.Sigmoid, scale=1.702).then_inc(sig_done, 1)
                    if half == 0:
                        act.wait_ge(hidT_ps, 2 * i + 2)
                        a.activation(hidT[:, 0:4, :], ps[:, 6, 0:4 * CAP].rearrange("p (k n) -> p k n", n=CAP),
                                     ACT.Copy).then_inc(hidT_ready, 1)
                act.wait_ge(hidT_ps, 2 * i + 3)
                a.activation(hidT[:, 4:8, :], ps[:, 7, 0:4 * CAP].rearrange("p (k n) -> p k n", n=CAP),
                             ACT.Copy).then_inc(hidT_ready, 1)
                act.wait_ge(y_ps, i + 1)
                act.wait_ge(gate_ready, i + 1)
                act.wait_ge(idx_kept, i + 1)
                for t in range(2):
                    a.activation(ysb[:, t * 512:(t + 1) * 512], ps[0:CAP, 4 + t, :], ACT.Copy,
                                 scale=gate_c[:, 0:1]).then_inc(y_ready, 1)

            act.dma_start(gfin, g_final.rearrange("(l n) -> l n", l=1).to_broadcast([128, D])).then_inc(gfin_in, 16)
            for c in range(NT):
                act.wait_ge(acc_in[c], 16)
                a.activation(xn[:, c, :], xs[:, c, :], ACT.Square, accum_out=ss[:, c:c + 1]).then_inc(fsq_done, 1)
                act.wait_ge(fsq_done, c + 1)
                a.activation(ss[:, c:c + 1], ss[:, c:c + 1], ACT.Sqrt, bias=eps[:, 0:1],
                             scale=1.0 / D).then_inc(frt_done, 1)

        @block.vector
        def _(dve):
            v = nc.vector
            steps = [0]

            def link(ins):
                steps[0] += 1
                ins.then_inc(dve_step, 1)
                dve.wait_ge(dve_step, steps[0])

            dve.wait_ge(gcol_ps, 1)
            v.tensor_copy(gcol[:, 0:16], ps[:, 7, 0:16])
            v.tensor_copy(gcol[:, 16:24].rearrange("p (b k) -> p b k", k=2),
                          ps[:, 7, 16:24].rearrange("p (k b) -> p b k", k=2)).then_inc(gcol_ready, 1)
            for c in range(NT):
                dve.wait_ge(rt_done, c + 1)
                link(v.reciprocal(rstd[:, c:c + 1], ss[:, c:c + 1]))
                v.tensor_scalar(xn[:, c, :], xs[:, c, :], rstd[:, c:c + 1], None, ALU.mult).then_inc(xn_ready, 1)
            dve.wait_ge(gcol_ready, 1)
            for k in range(1, KD, 2):
                dve.wait_ge(hT_ps, k + 1)
                v.tensor_scalar(hT[:, k, :], ps[:, k, :], gcol[:, k:k + 1], None, ALU.mult).then_inc(hT_d, 1)
            dve.wait_ge(consts_in, 144)
            for c in range(NT):
                dve.wait_ge(proj_out, 8 + c + 1)
                if c:
                    dve.wait_ge(rope_done, c)
                qa = qk[:, c, 0:768].rearrange("p (h n) -> p h n", n=HD)
                link(v.tensor_tensor(rt1, qk[:, c, 0:768], qk[:, c, 0:768], ALU.mult))
                v.tensor_reduce(hs[:, c, :], rt1.rearrange("p (h n) -> p h n", n=HD), AX.X,
                                ALU.add).then_inc(hs_ready, 1)
                dve.wait_ge(hrt_done, c + 1)
                link(v.reciprocal(hs[:, c, :], hs[:, c, :]))
                link(v.tensor_tensor(qa, qa, hs[:, c, :].unsqueeze(2).to_broadcast([128, 12, HD]), ALU.mult))
                v.tensor_tensor(qa[:, 0:8, :], qa[:, 0:8, :],
                                gains[:, 0:1, :].to_broadcast([128, 8, HD]), ALU.mult)
                link(v.tensor_tensor(qa[:, 8:12, :], qa[:, 8:12, :],
                                     gains[:, 1:2, :].to_broadcast([128, 4, HD]), ALU.mult))
                last = None
                for br in range(2):
                    h = qk[:, c, br * 768:(br + 1) * 768].rearrange("p (h two n) -> p h two n", two=2, n=32)
                    x1, x2 = h[:, :, 0, :], h[:, :, 1, :]
                    cos = rp[:, c, 2 * br:2 * br + 1, :].to_broadcast([128, 12, 32])
                    sin = rp[:, c, 2 * br + 1:2 * br + 2, :].to_broadcast([128, 12, 32])
                    t1 = rt1[:, br * 384:(br + 1) * 384].rearrange("p (h n) -> p h n", n=32)
                    t2 = rt2[:, br * 384:(br + 1) * 384].rearrange("p (h n) -> p h n", n=32)
                    v.tensor_tensor(t1, x1, sin, ALU.mult)
                    link(v.tensor_tensor(t2, x2, sin, ALU.mult))
                    v.tensor_tensor(x1, x1, cos, ALU.mult)
                    link(v.tensor_tensor(x2, x2, cos, ALU.mult))
                    v.tensor_tensor(x1, x1, t2, ALU.subtract)
                    last = v.tensor_tensor(x2, x2, t1, ALU.add)
                last.then_inc(rope_done, 1)
            for n in range(0, 12, 2):
                dve.wait_ge(qT_ps, n + 1)
                c, t = n // 3, n % 3
                v.tensor_copy(qT[:, 4 * t:4 * t + 4, c * 128:(c + 1) * 128],
                              ps[:, 4 + t, :].rearrange("p (t n) -> p t n", n=128)).then_inc(qT_d, 1)

            def row_max(j):
                w = SEQ if j < 8 else WW
                dve.wait_ge(scores_ps, j + 1)
                if j:
                    dve.wait_ge(negm_ready, j)
                link(v.reduce_max(mx[:, :], ps[:, 0:4, 0:w], AX.X))
                if j < 8:
                    v.tensor_scalar(negm[:, j % 2, :], mx[:, :], -SCALE, None, ALU.mult).then_inc(negm_ready, 1)
                else:
                    link(v.tensor_scalar(mx[:, :], mx[:, :], SCALE, sink[:, j - 8:j - 7], ALU.mult, ALU.max))
                    v.tensor_scalar(negm[:, j % 2, :], mx[:, :], -1.0, None, ALU.mult).then_inc(negm_ready, 1)

            def diagonals(j):
                dve.wait_ge(exps_done, 4 * j + 4)
                total = psum_p[:, j % 2, :]
                if j >= 8:
                    dve.wait_ge(esink_done, j - 7)
                    link(v.tensor_tensor(total, total, esink[:, j % 2, :], ALU.add))
                if j:
                    dve.wait_ge(diag_ready, j)
                link(v.reciprocal(rinv[:, :], total))
                if j:
                    dve.wait_ge(pT_ps, 4 * j)
                for n in range(4):
                    last = v.tensor_scalar(diag[:, n, :], ident[:, :], rinv[:, n:n + 1], None, ALU.mult)
                last.then_inc(diag_ready, 1)

            row_max(0)
            diagonals(0)
            for j in range(JOBS):
                if j + 1 < JOBS:
                    row_max(j + 1)
                for kb in range(2, 4):
                    dve.wait_ge(pT_ps, 4 * j + kb + 1)
                    if j:
                        dve.wait_ge(pv_ps, j)
                    q0, q1 = (0, NT) if j < 8 else (window(kb)[0], window(kb)[-1] + 1)
                    v.tensor_copy(pT[:, kb, q0 * 128:q1 * 128],
                                  ps[:, 4 + (4 * j + kb) % 3, q0 * 128:q1 * 128]).then_inc(pT_d, 1)
                if j + 1 < JOBS:
                    diagonals(j + 1)
                if j % 2:
                    dve.wait_ge(pv_ps, j + 1)
                    v.tensor_copy(oT[:, j // 2, :], ps[:, 7, :]).then_inc(oT_out, 1)

            for c in range(KD):
                dve.wait_ge(branch_ps, c + 1)
                b = (c % 2) * 2
                if c >= 2:
                    dve.wait_ge(merged, c - 1)
                v.tensor_tensor(mT[:, c, :], gT[:, c, :], ps[:, b, :], ALU.mult)
                link(v.tensor_tensor(mtmp[:, c % 2, :], gT[:, 8 + c, :], ps[:, b + 1, :], ALU.mult))
                v.tensor_tensor(mT[:, c, :], mT[:, c, :], mtmp[:, c % 2, :], ALU.add).then_inc(merged, 1)

            def residual(c):
                for t in range(2):
                    n = 2 * c + t
                    dve.wait_ge(wout_ps, n + 1)
                    half = xs[:, c, t * 512:(t + 1) * 512]
                    v.tensor_tensor(half, half, ps[:, 4 + n % 4, :], ALU.add).then_inc(x1_ready, 1)
                dve.wait_ge(rt2_done, c + 1)
                v.reciprocal(rstd[:, c:c + 1], ss[:, c:c + 1]).then_inc(rstd2_ready, 1)

            def h2_out(c):
                dve.wait_ge(h2T_ps, c + 1)
                if c >= 2:
                    dve.wait_ge(logits_ps, c - 1)
                for t in range(2):
                    last = v.tensor_tensor(h2T[:, c % 2, 4 * t:4 * t + 4, :],
                                           ps[:, t, :].rearrange("p (k n) -> p k n", n=128),
                                           gcol[:, 8 + 4 * t:12 + 4 * t].unsqueeze(2).to_broadcast([128, 4, 128]),
                                           ALU.mult)
                last.then_inc(h2T_out, 1)

            def choose(c):
                dve.wait_ge(logits_ps, c + 1)
                link(v.tensor_tensor(lg[:, c, :], ps[:, 2, c * E:(c + 1) * E], brt[:, :], ALU.add))
                if c:
                    dve.wait_ge(lg_ready, c)
                link(v.max(m8[:, :], lg[:, c, :]))
                v.tensor_scalar(negl[:, c:c + 1], m8[:, 0:1], -1.0, None, ALU.mult).then_inc(lg_ready, 1)
                link(v.tensor_copy(m8x[:, 0:TOPK], m8[:, 0:TOPK]))
                link(v.match_replace(out=repl[:, :], in_to_replace=m8x[:, :], in_values=lg[:, c, :],
                                     imm_value=-3e38))
                v.tensor_scalar(mask[:, c, :], repl[:, :], -3e38, None, ALU.is_equal).then_inc(mask_ready, 1)
                dve.wait_ge(ex_done, c + 1)
                dve.wait_ge(mask_ready, c + 1)
                link(v.tensor_tensor(ex[:, c, :], ex[:, c, :], mask[:, c, :], ALU.mult))
                link(v.tensor_reduce(gsum[:, :], ex[:, c, :], AX.X, ALU.add))
                link(v.reciprocal(gsum[:, :], gsum[:, :]))
                link(v.tensor_scalar(ex[:, c, :], ex[:, c, :], gsum[:, 0:1], None, ALU.mult))
                for part in range(3, 6):
                    link(v.tensor_copy(feats[:, c, :, part], ex[:, c, :]))
                    if part < 5:
                        link(v.tensor_tensor(ex[:, c, :], ex[:, c, :], feats[:, c, :, part], ALU.subtract))

            link(v.memset(m8x[:, :], 3e38))
            residual(0)
            residual(1)
            h2_out(0)
            residual(2)
            choose(0)
            h2_out(1)
            residual(3)
            choose(1)
            h2_out(2)
            h2_out(3)
            choose(2)
            choose(3)
            dve.wait_ge(pos_ps, 1)
            link(v.scalar_tensor_tensor(out=posx[:, :, :], in0=ps[:, 3, 0:128].rearrange("p (c e) -> p c e", e=E),
                                        scalar=1024.0, in1=mask[:, :, :], op0=ALU.add, op1=ALU.mult))
            v.tensor_scalar(posx[:, :, :], posx[:, :, :], -1024.0, None, ALU.add).then_inc(route_ready, 1)
            link(v.reduce_max(cmax[:, :], ps[:, 3, 128:160], AX.X))
            link(v.tensor_scalar(over[:, 0:PASSES - 1], passoff[:, 1:PASSES], cmax[:, 0:1], None, ALU.is_lt))
            link(v.tensor_reduce(npass[:, :], over[:, 0:PASSES - 1], AX.X, ALU.add))
            v.tensor_scalar(items_i[:, :], npass[:, :], 1.0, float(E), ALU.add, ALU.mult).then_inc(items_ready, 1)
            dve.wait_ge(items_ready, 1)
            items = dve.value_load(items_i[0:1, 0:1], min_val=E, max_val=E * PASSES)
            dve.wait_ge(route_ready, 1)

            base = steps[0]

            def serve(i, n_link):
                e, b = i % E, i // E
                v.tensor_scalar(tgt[:, :], posx[:, :, bass.ds(e, 1)].rearrange("p c one -> p (c one)"),
                                passoff[:, bass.ds(b, 1)], None, ALU.subtract).then_inc(dve_step, 1)
                dve.wait_ge(dve_step, n_link)
                v.tensor_tensor(onehot[:, :, :], iota_cap[:, :].unsqueeze(1).to_broadcast([128, NT, CAP]),
                                tgt[:, :].unsqueeze(2).to_broadcast([128, NT, CAP]),
                                ALU.is_equal).then_inc(onehot_ready, 1)

            def index(n, n_link, n_ready=None):
                dve.wait_ge(idx_done, n)
                v.tensor_copy(f6[:, :], idx_ps).then_inc(dve_step, 1)
                dve.wait_ge(dve_step, n_link)
                if n_ready is not None:
                    dve.wait_ge(idx_ready, n_ready)
                v.tensor_reduce(s1[:, :], f6[:, 0:2], AX.X, ALU.add)
                v.tensor_tensor(s2[:, :], f6[:, 2:3], idle_neg[0:CAP, :], ALU.mult).then_inc(dve_step, 1)
                dve.wait_ge(dve_step, n_link + 1)
                v.scalar_tensor_tensor(out=idx_g[:, :], in0=s2[:, :], scalar=idle_row[0:CAP, 0:1], in1=s1[:, :],
                                       op0=ALU.add, op1=ALU.add).then_inc(idx_ready, 1)

            def rows_out(n):
                dve.wait_ge(xt_ps, n)
                for t in range(2):
                    last = v.tensor_tensor(XT[:, 4 * t:4 * t + 4, :],
                                           ps[:, t, 0:4 * CAP].rearrange("p (k n) -> p k n", n=CAP),
                                           gcol[:, 16 + 4 * t:20 + 4 * t].unsqueeze(2).to_broadcast([128, 4, CAP]),
                                           ALU.mult)
                last.then_inc(xt_ready, 1)

            def per_item(i):
                e = i % E
                v.tensor_scalar(sel[:, :], part_mod[:, :], erow[:, bass.ds(e, 1)], None,
                                ALU.is_equal).then_inc(sel_ready, 1)
                v.tensor_reduce(gate_c[:, :], f6[:, 3:6], AX.X, ALU.add).then_inc(gate_ready, 1)

            serve(0, base + 1)
            index(1, base + 2)
            v.tensor_scalar(sel[:, :], part_mod[:, :], erow[:, 0:1], None, ALU.is_equal).then_inc(sel_ready, 1)
            v.tensor_reduce(gate_c[:, :], f6[:, 3:6], AX.X, ALU.add).then_inc(gate_ready, 1)
            rows_out(1)
            PER = 7
            dve.sem_inc(hid_ready, 1)
            with dve.Fori(0, items) as i:
                at = i * PER + base + 3
                dve.wait_ge(idx_done, i + 1)
                serve(i + 1, at + 1)
                for half in range(2):
                    b = 2 * half
                    dve.wait_ge(pair_ps, 2 * i + half + 1)
                    dve.wait_ge(hid_ready, 2 * i + half + 1)
                    v.tensor_scalar(gc, ps[0:CAP, b, :], 7.0, None, ALU.min).then_inc(clamp_ready, 1)
                    v.tensor_scalar(uc, ps[0:CAP, b + 1, :], 7.0, -7.0, ALU.min, ALU.max).then_inc(dve_step, 1)
                    dve.wait_ge(dve_step, at + (2 if half == 0 else 6))
                    dve.wait_ge(clamp_ready, 2 * i + half + 1)
                    v.scalar_tensor_tensor(out=uc, in0=uc, scalar=1.0, in1=gc, op0=ALU.add,
                                           op1=ALU.mult).then_inc(dve_step, 1)
                    dve.wait_ge(dve_step, at + (3 if half == 0 else 7))
                    dve.wait_ge(sig_done, 2 * i + half + 1)
                    if half == 0:
                        dve.wait_ge(hidT_ps, 2 * i + 1)
                    v.tensor_tensor(hid[:, half * 512:(half + 1) * 512], uc, sg, ALU.mult).then_inc(hid_ready, 1)
                    if half == 0:
                        dve.wait_ge(idx_kept, i + 1)
                        dve.wait_ge(gate_ready, i + 1)
                        index(i + 2, at + 4, i + 1)
                rows_out(i + 2)
                dve.wait_ge(down_begun, i + 1)
                dve.wait_ge(y_ready, 2 * i + 3)
                per_item(i + 1)

            dve.wait_ge(gfin_in, 16)
            fin = items * PER + base + 3
            for c in range(NT):
                dve.wait_ge(frt_done, c + 1)
                v.reciprocal(rstd[:, c:c + 1], ss[:, c:c + 1]).then_inc(dve_step, 1)
                dve.wait_ge(dve_step, fin + c + 1)
                v.scalar_tensor_tensor(out=xs[:, c, :], in0=xs[:, c, :], scalar=rstd[:, c:c + 1], in1=gfin,
                                       op0=ALU.mult, op1=ALU.mult).then_inc(out_ready, 1)

        @block.tensor
        def _(pe):
            t_ = nc.tensor
            mm = t_.matmul
            pe.wait_ge(pool_consts, 1)
            pe.wait_ge(consts_in, 144)
            t_.transpose(ps[:, 7, 0:16], g16[:, :], ident[0:16, 0:16])
            for k in range(2):
                last = t_.transpose(ps[:, 7, 16 + 4 * k:20 + 4 * k], g4[:, k:256:2], ident[0:4, 0:4])
            last.then_inc(gcol_ps, 1)
            pe.wait_ge(gcol_ready, 1)
            for c in range(NT):
                pe.wait_ge(xn_ready, c + 1)
                for k in range(KD):
                    last = t_.transpose(ps[:, k, c * 128:(c + 1) * 128], xn[:, c, k * 128:(k + 1) * 128], ident[:, :])
                    if c == NT - 1:
                        last.then_inc(hT_ps, 1)
            pe.wait_ge(hT_a, KD // 2)
            pe.wait_ge(hT_d, KD // 2)
            for grp in range(7):
                wait_chunk(pe, 2 * grp)
                wait_chunk(pe, 2 * grp + 1)
                for c in range(4):
                    n = 4 * grp + c
                    if n >= 4:
                        pe.wait_ge(proj_out, n - 3)
                    for k in range(KD):
                        w = chunk(2 * grp + k // 4, 512)[:, k % 4, :]
                        if grp < 3:
                            last = mm(ps[:, n % 4, :], hT[:, k, c * 128:(c + 1) * 128], w,
                                      start=(k == 0), stop=(k == KD - 1))
                        else:
                            last = mm(ps[:, n % 4, :], w[:, c * 128:(c + 1) * 128], hT[:, k, :],
                                      start=(k == 0), stop=(k == KD - 1))
                    last.then_inc(proj_ps, 1)
                pe.wait_ge(proj_ps, 4 * grp + 4)
                pe.sem_inc(chunks_used, 2)
            for n in range(12):
                c, t = n // 3, n % 3
                if t == 0:
                    pe.wait_ge(rope_done, c + 1)
                if n >= 3:
                    pe.wait_ge(qT_a if n % 2 == 0 else qT_d, (n - 3) // 2 + 1)
                for u in range(4):
                    col = (4 * t + u) * 128
                    last = t_.transpose(ps[:, 4 + t, u * 128:(u + 1) * 128], qk[:, c, col:col + 128], ident[:, :])
                last.then_inc(qT_ps, 1)
            pe.wait_ge(qT_a, 6)
            pe.wait_ge(qT_d, 6)
            pe.wait_ge(proj_out, 28)

            def scores(j):
                br, h = j // 8, j % 8
                if j:
                    pe.wait_ge(exps_done, 4 * j)
                r = slice(64 * (h % 2), 64 * (h % 2) + 64)
                q, k = qT[r, 6 * br + h // 2, :], qT[r, 6 * br + 4 + h // 4, :]
                for n in range(NT):
                    qn = q[:, n * 128:(n + 1) * 128]
                    if br == 0:
                        last = mm(ps[:, n, :], qn, k, start=True, stop=True)
                        continue
                    w = window(n)
                    c0 = (w[0] - n + 1) * 128
                    mm(ps[:, n, c0:c0 + 128 * len(w)], qn, k[:, w[0] * 128:(w[-1] + 1) * 128], start=True, stop=False)
                    mm(ps[:, n, 0:128], identb[:, :], (mask_lo if n else mask_all)[:, :], start=False, stop=False)
                    last = mm(ps[:, n, 256:384], identb[:, :], (mask_hi if n < NT - 1 else mask_all)[:, :],
                              start=False, stop=True)
                last.then_inc(scores_ps, 1)

            def values(j):
                br, h = j // 8, j % 8
                pe.wait_ge(diag_ready, j + 1)
                for kb in range(NT):
                    m = 4 * j + kb
                    old = m - 3
                    if old >= 0:
                        oj, okb = old // 4, old % 4
                        if okb < 2:
                            pe.wait_ge(pT_a, 2 * oj + okb + 1)
                        else:
                            pe.wait_ge(pT_d, 2 * oj + okb - 1)
                    for n in (range(NT) if br == 0 else window(kb)):
                        c0 = kb * 128 if br == 0 else (kb - n + 1) * 128
                        last = mm(ps[:, 4 + m % 3, n * 128:(n + 1) * 128], probs[:, j % 2, n, c0:c0 + 128],
                                  diag[:, n, :], start=True, stop=True)
                    last.then_inc(pT_ps, 1)
                vc = br * 128 + (h // 4) * 64
                o = ps[64 * (h % 2):64 * (h % 2) + 64, 7, :]
                if h % 2 == 0 and j:
                    pe.wait_ge(oT_out, j // 2)
                if br == 0:
                    for kb in range(NT):
                        if kb < 2:
                            pe.wait_ge(pT_a, 2 * j + kb + 1)
                        else:
                            pe.wait_ge(pT_d, 2 * j + kb - 1)
                        last = mm(o, v_sb[:, kb, vc:vc + 64], pT[:, kb, :], start=(kb == 0), stop=(kb == NT - 1))
                else:
                    pe.wait_ge(pT_a, 2 * j + 2)
                    for n in range(NT):
                        pe.wait_ge(pT_d, 2 * j + (1 if n < 2 else 2))
                        w = window(n)
                        for kb in w:
                            last = mm(o[:, n * 128:(n + 1) * 128], v_sb[:, kb, vc:vc + 64],
                                      pT[:, kb, n * 128:(n + 1) * 128], start=(kb == w[0]), stop=(kb == w[-1]))
                last.then_inc(pv_ps, 1)

            scores(0)
            for j in range(JOBS):
                if j + 1 < JOBS:
                    scores(j + 1)
                values(j)

            pe.wait_ge(oT_out, 8)
            for n in range(BR_A, W_OUT):
                wait_chunk(pe, n)
            for c in range(KD):
                if c >= 2:
                    pe.wait_ge(merged, c - 1)
                for br in range(2):
                    for k in range(4):
                        w = chunk((BR_A, BR_B)[br] + k // 2, D)[:, k % 2, c * 128:(c + 1) * 128]
                        last = mm(ps[:, (c % 2) * 2 + br, :], w, oT[:, 4 * br + k, :], start=(k == 0), stop=(k == 3))
                last.then_inc(branch_ps, 1)
            pe.wait_ge(branch_ps, KD)
            pe.sem_inc(chunks_used, W_OUT - BR_A)
            pe.wait_ge(merged, KD)
            for n in range(W_OUT, CHUNKS):
                wait_chunk(pe, n)

            def out_proj(c):
                for t in range(2):
                    n = 2 * c + t
                    if n >= 4:
                        pe.wait_ge(x1_ready, n - 3)
                    for k in range(KD):
                        last = mm(ps[:, 4 + n % 4, :], mT[:, k, c * 128:(c + 1) * 128],
                                  chunk(W_OUT + k // 2, D)[:, k % 2, t * 512:(t + 1) * 512],
                                  start=(k == 0), stop=(k == KD - 1))
                    last.then_inc(wout_ps, 1)

            def h2_transpose(c):
                pe.wait_ge(xn2_ready, c + 1)
                if c:
                    pe.wait_ge(h2T_out, c)
                for k in range(KD):
                    last = t_.transpose(ps[:, k // 4, (k % 4) * 128:(k % 4 + 1) * 128],
                                        xn[:, c, k * 128:(k + 1) * 128], ident[:, :])
                last.then_inc(h2T_ps, 1)

            def router(c):
                pe.wait_ge(h2T_out, c + 1)
                if c:
                    pe.wait_ge(lg_ready, c)
                for k in range(KD):
                    last = mm(ps[:, 2, c * E:(c + 1) * E], h2T[:, c % 2, k, :], wr[:, k, :],
                              start=(k == 0), stop=(k == KD - 1))
                last.then_inc(logits_ps, 1)

            out_proj(0)
            out_proj(1)
            h2_transpose(0)
            out_proj(2)
            router(0)
            h2_transpose(1)
            out_proj(3)
            pe.wait_ge(wout_ps, 2 * NT)
            pe.sem_inc(chunks_used, CHUNKS - W_OUT)
            router(1)
            h2_transpose(2)
            router(2)
            h2_transpose(3)
            router(3)
            for c in range(NT):
                pe.wait_ge(mask_ready, c + 1)
                for d in range(c + 1):
                    mm(ps[:, 3, c * E:(c + 1) * E], (tri if d == c else onesb)[:, :], mask[:, d, :],
                       start=(d == 0), stop=(d == c))
            for d in range(NT):
                last = mm(ps[:, 3, 128:128 + E], onesb[:, :], mask[:, d, :], start=(d == 0), stop=(d == NT - 1))
            last.then_inc(pos_ps, 1)

            def slots(i, n):
                pe.wait_ge(onehot_ready, n)
                pe.wait_ge(hidT_ready, 2 * i - 1)
                for c in range(NT):
                    last = mm(idx_ps, onehot[:, c, :], feats[:, c, bass.ds(i % E, 1), :].rearrange("p one f -> p (one f)"),
                              start=(c == 0), stop=(c == NT - 1))
                last.then_inc(idx_done, 1)

            def rows_in(n):
                pe.wait_ge(gathered, n * 16)
                for k in range(KD):
                    last = t_.transpose(ps[:, k // 4, (k % 4) * CAP:(k % 4 + 1) * CAP],
                                        xg[:, (k // 2) * 256 + k % 2:(k // 2 + 1) * 256:2], ident[0:CAP, 0:CAP])
                last.then_inc(xt_ps, 1)

            pe.wait_ge(items_ready, 1)
            items = pe.value_load(items_i[0:1, 0:1], min_val=E, max_val=E * PASSES)
            pe.wait_ge(onehot_ready, 1)
            for c in range(NT):
                last = mm(idx_ps, onehot[:, c, :], feats[:, c, 0, :], start=(c == 0), stop=(c == NT - 1))
            last.then_inc(idx_done, 1)
            rows_in(1)
            pe.wait_ge(bias_ready, 1)
            pe.sem_inc(hidT_ps, 1)
            with pe.Fori(0, items) as i:
                pe.wait_ge(xt_ready, i + 1)
                for half in range(2):
                    b = 2 * half
                    if half:
                        slots(i + 1, i + 2)
                        pe.wait_ge(hid_ready, 2 * i + 1)
                    for s in range(4 * half, 4 * half + 4):
                        pe.wait_ge(slot_full[s], (i + loads_before[s] + 1) * 16)
                        for k in range(2):
                            for t in range(2):
                                last = mm(ps[0:CAP, b + t, :], XT[:, 2 * (s % 4) + k, :], expert_w(s, k, t),
                                          start=(s % 4 == 0 and k == 0), stop=False)
                        last.then_inc(item_chunks_used, 1)
                    pe.wait_ge(sel_ready, i + 1)
                    for t in range(2):
                        col = t * FF + half * 512
                        last = mm(ps[0:CAP, b + t, :], sel[:, :], bias_tab[:, col:col + 512], start=False, stop=True)
                    last.then_inc(pair_ps, 1)

                def hidden_T(half):
                    pe.wait_ge(hid_ready, 2 * i + half + 2)
                    if half:
                        pe.wait_ge(idx_ready, i + 2)
                    for k in range(4):
                        last = t_.transpose(ps[:, 6 + half, k * CAP:(k + 1) * CAP],
                                            hid[:, half * 512 + k * 128:half * 512 + (k + 1) * 128],
                                            ident[0:CAP, 0:CAP])
                    last.then_inc(hidT_ps, 1)

                hidden_T(0)
                rows_in(i + 2)
                pe.wait_ge(y_ready, 2 * i + 1)
                for t in range(2):
                    col = 2 * FF + t * 512
                    last = mm(ps[0:CAP, 4 + t, :], sel[:, :], bias_tab[:, col:col + 512], start=True, stop=False)
                last.then_inc(down_begun, 1)
                for half in range(2):
                    if half:
                        hidden_T(1)
                    pe.wait_ge(hidT_ready, 2 * i + half + 2)
                    for s in range(8 + 2 * half, 10 + 2 * half):
                        pe.wait_ge(slot_full[s], (i + loads_before[s] + 1) * 16)
                        for k in range(2):
                            for t in range(2):
                                last = mm(ps[0:CAP, 4 + t, :], hidT[:, 2 * (s - 8) + k, :], expert_w(s, k, t),
                                          start=False, stop=(s == 11 and k == 1))
                        last.then_inc(item_chunks_used, 1)
                pe.wait_ge(item_chunks_used, (i + 1) * NSLOT)
                pe.sem_inc(y_ps, 1)


_INS = ['x', 'g_mix', 'w_in', 'qa_norm', 'ka_norm', 'sink_b', 'w_branch_a', 'w_branch_b', 'w_out', 'g_ffn', 'w_router',
        'b_router', 'w_gate_up', 'b_gate_up', 'w_down', 'b_down', 'g_final']


def rope_tables():
    grid = 64
    t = np.arange(SEQ)
    inv_ax = np.float32(10000.0) ** (-np.arange(0, HD // 2, 2, dtype=np.float32) / np.float32(HD // 2))
    inv_1d = np.float32(10000.0) ** (-np.arange(0, HD, 2, dtype=np.float32) / np.float32(HD))
    row, col = (t // grid).astype(np.float32), (t % grid).astype(np.float32)
    ax = np.concatenate([row[:, None] * inv_ax, col[:, None] * inv_ax], axis=-1).astype(np.float32)
    d1 = (t.astype(np.float32)[:, None] * inv_1d).astype(np.float32)
    return np.stack([np.cos(ax), np.sin(ax), np.cos(d1), np.sin(d1)], axis=1).astype(np.float32)


def kernel(**inputs):
    import concourse.bacc as _bacc
    from concourse.bass_utils import run_bass_kernel_spmd as _run

    nc = _bacc.Bacc("TRN2", target_bir_lowering=False, num_devices=1)
    f32 = mybir.dt.float32
    arrays, args = {}, []
    for name in _INS:
        a = np.ascontiguousarray(inputs[name])
        arrays[f"in_{name}"] = a
        args.append(nc.dram_tensor(f"in_{name}", a.shape, mybir.dt.from_np(a.dtype), kind="ExternalInput").ap())
    tables = rope_tables()
    arrays["rope_tables"] = tables
    args.append(nc.dram_tensor("rope_tables", tables.shape, f32, kind="ExternalInput").ap())
    args.append(nc.dram_tensor("h2_rows", (SEQ + CAP, D), f32, kind="Internal").ap())
    args.append(nc.dram_tensor("sum_rows", (SEQ + CAP, D), f32, kind="Internal").ap())
    args.append(nc.dram_tensor("out", (1, SEQ, D), f32, kind="ExternalOutput").ap())
    encoder_block(nc, *args)
    r = _run(nc, [arrays], core_ids=[0])
    return r.results[0]["out"]
```

```python
import numpy as np
import concourse.bass as bass
from concourse import mybir
from contextlib import ExitStack

SEQ, D, HD = 512, 1024, 64
NT, KD = SEQ // 128, D // 128
E, FF, TOPK = 32, 1024, 4
CAP = 96
PASSES = -(-SEQ // CAP)
EPS = 1e-6
SLOT = 2048
NRAW = 8
NSPLIT = 6
NIN, NIN_SPLIT = 4, 3
NCH = 12


def encoder_block(nc, x, g_mix, w_in, qa_norm, ka_norm, sink_b, w_branch_a, w_branch_b, w_out, g_ffn, w_router,
                  b_router, w_gate_up, b_gate_up, w_down, b_down, g_final, rope, h2buf, acc, out):
    F32, BF16, I32, F32R = mybir.dt.float32, mybir.dt.bfloat16, mybir.dt.int32, mybir.dt.float32r
    ALU, ACT, AX = mybir.AluOpType, mybir.ActivationFunctionType, mybir.AxisListType
    NEG = -1e30
    ROWS = SEQ + CAP
    JOBS = 16
    SCALE = HD ** -0.5

    ctx = ExitStack()
    with ctx:
        def sb(name, shape, dt=F32):
            return ctx.enter_context(nc.sbuf_tensor(name, shape, dt))

        def sem(name):
            return ctx.enter_context(nc.semaphore(name))

        ARENA = (nc.sbuf_usable_end - 196 * 1024) // 32 * 32

        def at(name, kib, shape, dt=F32):
            return nc.alloc_sbuf_tensor_at(name, shape, dt, offset=ARENA + int(kib * 1024))

        raw = at("raw", 0, [128, NRAW, SLOT])
        gT = at("gates_T", 32, [128, 16, SEQ])
        zeros = at("zeros", 32, [CAP, D])
        wo = at("w_out_raw", 64, [128, 4, SLOT])
        split = at("split", 64, [128, NSPLIT, 2, SLOT], F32R)
        g16 = at("g16", 96, [16, 128])
        diag = at("diag", 96, [128, 4, 128])
        wr = at("w_router", 98, [128, KD, E])
        gffn = at("g_ffn_rows", 100, [128, D])
        hT = at("hT", 112, [128, 2, KD, SEQ], F32R)
        qT = at("qT", 112, [128, 12, SEQ])
        mT = at("merged_T", 112, [128, KD, SEQ])
        bias32 = at("bias32", 128, [128, 3 * D])
        oTa = at("oT_a", 136, [128, 4, SEQ])
        xs = at("xs", 144, [128, NT, D])
        xn = at("xn", 160, [128, NT, D])
        qk = at("qk", 160, [128, NT, 1536])
        probs = at("probs", 160, [128, 2, 4, 512])
        oTb = at("oT_b", 176, [128, 4, SEQ])
        h2T = at("h2T", 176, [128, 2, KD, 128])
        v_sb = at("v", 184, [128, NT, 256])
        rt1_t = at("rt1", 188, [128, 768])
        rt2_t = at("rt2", 191, [128, 768])
        pT = at("pT", 188, [128, 4, SEQ])
        mtmp = at("mtmp", 188, [128, 2, 512])
        bias_tab = at("bias_tab", 190, [128, 3 * D], BF16)
        xg_t = at("xg", 160, [CAP, D])
        hid_t = at("hid", 164, [CAP, FF])
        ysb_t = at("y", 168, [CAP, D])
        gc_t = at("gate_half", 172, [CAP, 512])
        uc_t = at("up_half", 174, [CAP, 512])
        sg_t = at("sig_half", 176, [CAP, 512])
        XT = at("XT", 178, [128, 2, KD, CAP], F32R)
        hidT = at("hidT", 184, [128, 2, KD, CAP], F32R)
        fin = at("fin", 0, [128, NT, D])
        fin_sq = at("fin_sq", 16, [128, NT, D])
        gfin_t = at("g_final_rows", 32, [128, D])
        rt1, rt2, gfin = rt1_t[:, :], rt2_t[:, :], gfin_t[:, :]
        xg, hid, ysb, gc, uc, sg = xg_t[:, :], hid_t[:, :], ysb_t[:, :], gc_t[:, :], uc_t[:, :], sg_t[:, :]

        ident = sb("ident", [128, 128])
        identb = sb("identb", [128, 128], BF16)
        mask_lo = sb("mask_lo", [128, 128], BF16)
        mask_hi = sb("mask_hi", [128, 128], BF16)
        mask_all = sb("mask_all", [128, 128], BF16)
        tri = sb("tri", [128, 128], BF16)
        onesb = sb("onesb", [128, 128], BF16)
        iota_cap = sb("iota_cap", [128, CAP])
        part_mod = sb("part_mod", [128, CAP])
        erow = sb("erow", [128, E])
        passoff = sb("passoff", [128, 8])
        idle_row = sb("idle_row", [128, 1])
        idle_neg = sb("idle_neg", [128, 1])
        feats = sb("feats", [128, NT, E, 6], BF16)
        shared = sb("shared", [128, 512])
        rp = shared[:, :].rearrange("p (c t n) -> p c t n", t=4, n=32)
        posx = shared[:, 0:128].rearrange("p (c e) -> p c e", e=E)
        ex = shared[:, 128:256].rearrange("p (c e) -> p c e", e=E)
        onehot = shared[:, 256:448].bitcast(BF16).rearrange("p (c n) -> p c n", n=CAP)
        gains = sb("gains", [128, 2, HD])
        sink = sb("sink", [128, 8])
        brt = sb("brt", [128, E])
        gcol = sb("gcol", [128, KD])
        eps = sb("eps", [128, 1])
        warm = sb("warm", [128, 1])
        ss = sb("ss", [128, NT])
        rstd = sb("rstd", [128, NT])
        hs = sb("hs", [128, NT, 12])
        mx = sb("mx", [128, 4])
        negm = sb("negm", [128, 2, 4])
        esink = sb("esink", [128, 2, 4])
        psum_p = sb("psum_p", [128, 2, 4])
        rinv = sb("rinv", [128, 4])
        lg = sb("lg", [128, NT, E])
        m8 = sb("m8", [128, 8])
        m8x = sb("m8x", [128, 8])
        repl = sb("repl", [128, E])
        mask = sb("mask", [128, NT, E], BF16)
        negl = sb("negl", [128, NT])
        gsum = sb("gsum", [128, NT])
        cmax = sb("cmax", [128, 1])
        over = sb("over", [128, 8])
        npass = sb("npass", [128, 1])
        items_i = sb("items_i", [128, 2], I32)
        tgt = sb("tgt", [128, NT])
        sel = sb("sel", [128, CAP], BF16)
        f6 = sb("f6", [CAP, 6])
        s1 = sb("s1", [CAP, 1])
        s2 = sb("s2", [CAP, 1])
        idx_g = sb("idx_g", [CAP, 1], I32)
        idx_s = sb("idx_s", [CAP, 1], I32)
        gate_c = sb("gate_c", [CAP, 1])

        assert nc.sbuf_base <= ARENA
        ps = ctx.enter_context(nc.psum_tensor("ps", [128, 8, 512], F32))
        idx_ps = ps[0:CAP, 7, 448:454]

        x_in = [sem(f"x_in{c}") for c in range(NT)]
        g_mix_in = sem("g_mix_in")
        consts_in = sem("consts_in")
        late_in = sem("late_in")
        chunk_in = [sem(f"chunk_in{s}") for s in range(NIN)]
        wo_in = [sem(f"wo_in{s}") for s in range(4)]
        expert_in = [sem(f"expert_in{s}") for s in range(NCH)]
        in_hi = sem("in_hi")
        in_lo = sem("in_lo")
        in_used = sem("in_used")
        branches_used = sem("branches_used")
        ex_hi = sem("ex_hi")
        ex_lo = sem("ex_lo")
        ex_used = sem("ex_used")
        pool_step = sem("pool_step")
        eps_set = sem("eps_set")
        ident_set = sem("ident_set")
        pool_past = sem("pool_past")
        zero_set = sem("zero_set")
        pool_consts = sem("pool_consts")
        part_mod_set = sem("part_mod_set")
        zeros_stored = sem("zeros_stored")
        gcol_ps = sem("gcol_ps")
        gcol_ready = sem("gcol_ready")
        sq_done = sem("sq_done")
        rt_done = sem("rt_done")
        dve_step = sem("dve_step")
        xn_ready = sem("xn_ready")
        hT_ps = sem("hT_ps")
        hT_hi = sem("hT_hi")
        hT_lo = sem("hT_lo")
        proj_ps = sem("proj_ps")
        proj_out = sem("proj_out")
        hs_ready = sem("hs_ready")
        hrt_done = sem("hrt_done")
        rope_done = sem("rope_done")
        qT_ps = sem("qT_ps")
        qT_a = sem("qT_a")
        qT_d = sem("qT_d")
        scores_ps = sem("scores_ps")
        negm_ready = sem("negm_ready")
        exps_done = sem("exps_done")
        esink_done = sem("esink_done")
        diag_ready = sem("diag_ready")
        pT_ps = sem("pT_ps")
        pT_a = sem("pT_a")
        pT_d = sem("pT_d")
        pv_ps = sem("pv_ps")
        oT_out = sem("oT_out")
        branch_ps = sem("branch_ps")
        merged = sem("merged")
        wout_ps = sem("wout_ps")
        x1_ready = sem("x1_ready")
        sq2_done = sem("sq2_done")
        rt2_done = sem("rt2_done")
        xn2_ready = sem("xn2_ready")
        rows_stored = sem("rows_stored")
        h2T_ps = sem("h2T_ps")
        h2T_a = sem("h2T_a")
        h2T_d = sem("h2T_d")
        logits_ps = sem("logits_ps")
        lg_ready = sem("lg_ready")
        ex_done = sem("ex_done")
        mask_ready = sem("mask_ready")
        pos_ps = sem("pos_ps")
        route_ready = sem("route_ready")
        items_ready = sem("items_ready")
        bias_in = sem("bias_in")
        bias_ready = sem("bias_ready")
        onehot_ready = sem("onehot_ready")
        idx_done = sem("idx_done")
        idx_ready = sem("idx_ready")
        idx_kept = sem("idx_kept")
        gathered = sem("gathered")
        scattered = sem("scattered")
        xt_ps = sem("xt_ps")
        xt_hi = sem("xt_hi")
        xt_lo = sem("xt_lo")
        sel_ready = sem("sel_ready")
        gate_ready = sem("gate_ready")
        pair_ps = sem("pair_ps")
        clamp_ready = sem("clamp_ready")
        sig_done = sem("sig_done")
        hid_ready = sem("hid_ready")
        hidT_ps = sem("hidT_ps")
        hidT_hi = sem("hidT_hi")
        hidT_lo = sem("hidT_lo")
        down_begun = sem("down_begun")
        y_ps = sem("y_ps")
        y_ready = sem("y_ready")
        acc_in = [sem(f"acc_in{c}") for c in range(NT)]
        gfin_in = sem("gfin_in")
        fsq_done = sem("fsq_done")
        frt_done = sem("frt_done")
        out_ready = sem("out_ready")
        out_stored = sem("out_stored")

        def kp(ap):
            return ap.rearrange("(k p) n -> p k n", p=128)

        IN_CHUNKS, CHUNKS = 14, 18
        chunk_src = [kp(w_in[0, s * 512:(s + 1) * 512, g * 512:(g + 1) * 512]) for g in range(7) for s in range(2)]
        chunk_src += [kp(w[0, s * 256:(s + 1) * 256, :]) for w in (w_branch_a, w_branch_b) for s in range(2)]

        def blocks(t, width):
            return t.rearrange("p (k n) -> p k n", n=width)

        def expert_src(e, s):
            if s < 8:
                half, k2 = s // 4, s % 4
                w = w_gate_up[0, e, k2 * 256:(k2 + 1) * 256, :].rearrange("(p k) (t n) -> p (k t) n", k=2, t=2)
                return w[:, :, half * 512:(half + 1) * 512]
            return w_down[0, e, (s - 8) * 256:(s - 7) * 256, :].rearrange("(p k) n -> p (k n)", k=2)

        def raw_slot(i, s):
            n = (i * NCH + s) % NRAW
            return raw[:, n, :] if isinstance(n, int) else raw[:, bass.ds(n, 1), :].rearrange("p one n -> p (one n)")

        def load_expert(sp, i, s, e):
            dst = raw_slot(i, s)
            if s < 8:
                dst = dst.rearrange("p (a n) -> p a n", a=4)
            sp.dma_start(dst, expert_src(e, s)).then_inc(expert_in[s], 16)

        def expert_w(s, part, k, t):
            return split[:, s % NSPLIT, part, (2 * k + t) * 512:(2 * k + t + 1) * 512]

        def window(n):
            return [kb for kb in (n - 1, n, n + 1) if 0 <= kb < NT]

        WW = 384

        block = ctx.enter_context(nc.Block())

        @block.sync
        def _(sp):
            x_v = x.rearrange("b (c p) n -> (b c) p n", p=128)
            for c in range(NT):
                sp.dma_start(xs[:, c, :], x_v[c]).then_inc(x_in[c], 16)
            for n in range(CHUNKS):
                if n >= NIN:
                    sp.wait_ge(in_lo, n - NIN + 1)
                w = chunk_src[n]
                sp.dma_start(blocks(raw[:, n % NIN, :], w.shape[2]), w).then_inc(chunk_in[n % NIN], 16)
            sp.wait_ge(in_used, IN_CHUNKS)
            for s in range(4):
                sp.dma_start(blocks(wo[:, s, :], D), kp(w_out[0, s * 256:(s + 1) * 256, :])).then_inc(wo_in[s], 16)
            sp.wait_ge(branches_used, 1)
            for s in range(4):
                load_expert(sp, 0, s, 0)
            sp.wait_ge(merged, KD)
            for s in range(4, NRAW):
                load_expert(sp, 0, s, 0)
            for s in range(NRAW, NCH):
                sp.wait_ge(ex_lo, s - NRAW + 1)
                load_expert(sp, 0, s, 0)
            sp.wait_ge(items_ready, 1)
            items = sp.value_load(items_i[0:1, 0:1], min_val=E, max_val=E * PASSES)
            with sp.Fori(1, items) as i:
                for s in range(NCH):
                    sp.wait_ge(ex_lo, i * NCH + s - NRAW + 1)
                    load_expert(sp, i, s, i % E)
            sp.wait_ge(scattered, items * 16)
            acc_v = acc[0:SEQ, :].rearrange("(c p) n -> c p n", p=128)
            out_v = out.rearrange("b (c p) n -> (b c) p n", p=128)
            for c in range(NT):
                sp.dma_start(fin[:, c, :], acc_v[c]).then_inc(acc_in[c], 16)
            for c in range(NT):
                sp.wait_ge(out_ready, c + 1)
                sp.dma_start(out_v[c], fin[:, c, :]).then_inc(out_stored, 16)
            sp.wait_ge(out_stored, 16 * NT)

        @block.gpsimd
        def _(pool):
            g = nc.gpsimd
            g.memset(eps[:, :], EPS).then_inc(eps_set, 1)
            g.memset(ident[:, :], 0.0).then_inc(pool_step, 1)
            pool.wait_ge(pool_step, 1)
            g.affine_select(out=ident[:, :], in_=ident[:, :], compare_op=ALU.not_equal, fill=1.0, base=0,
                            pattern=[[-1, 128]], channel_multiplier=1).then_inc(ident_set, 1)
            g.memset(zeros[:, :], 0.0).then_inc(zero_set, 1)
            g.memset(identb[:, :], 0.0)
            g.memset(mask_lo[:, :], 0.0)
            g.memset(mask_hi[:, :], 0.0)
            g.memset(mask_all[:, :], NEG)
            g.memset(tri[:, :], 1.0)
            g.memset(onesb[:, :], 1.0)
            g.memset(part_mod[:, :], 999.0)
            g.memset(feats[:, :, :, 2:3], 1.0).then_inc(pool_step, 1)
            pool.wait_ge(pool_step, 2)
            g.affine_select(out=identb[:, :], in_=identb[:, :], compare_op=ALU.not_equal, fill=1.0, base=0,
                            pattern=[[-1, 128]], channel_multiplier=1)
            g.affine_select(out=mask_lo[:, :], in_=mask_lo[:, :], compare_op=ALU.is_ge, fill=NEG, base=0,
                            pattern=[[1, 128]], channel_multiplier=-1)
            g.affine_select(out=mask_hi[:, :], in_=mask_hi[:, :], compare_op=ALU.is_ge, fill=NEG, base=0,
                            pattern=[[-1, 128]], channel_multiplier=1)
            g.affine_select(out=tri[:, :], in_=tri[:, :], compare_op=ALU.is_ge, fill=0.0, base=-1,
                            pattern=[[1, 128]], channel_multiplier=-1)
            g.iota(iota_cap[:, :], pattern=[[1, CAP]], base=0, channel_multiplier=0,
                   allow_small_or_imprecise_dtypes=True)
            g.iota(erow[:, :], pattern=[[1, E]], base=0, channel_multiplier=0, allow_small_or_imprecise_dtypes=True)
            g.iota(passoff[:, :], pattern=[[CAP, 8]], base=0, channel_multiplier=0,
                   allow_small_or_imprecise_dtypes=True)
            g.iota(idle_row[:, :], pattern=[[0, 1]], base=SEQ, channel_multiplier=1,
                   allow_small_or_imprecise_dtypes=True)
            g.iota(idle_neg[:, :], pattern=[[0, 1]], base=-SEQ, channel_multiplier=-1,
                   allow_small_or_imprecise_dtypes=True)
            g.iota(feats[:, :, :, 0:1], pattern=[[0, NT], [0, E], [0, 1]], base=0, channel_multiplier=1,
                   allow_small_or_imprecise_dtypes=True)
            g.iota(feats[:, :, :, 1:2], pattern=[[128, NT], [0, E], [0, 1]], base=0, channel_multiplier=0,
                   allow_small_or_imprecise_dtypes=True).then_inc(pool_consts, 1)
            pool.wait_ge(pool_consts, 1)
            for q in range(3):
                g.iota(part_mod[32 * q:32 * q + 32, :], pattern=[[0, CAP]], base=0, channel_multiplier=1,
                       allow_small_or_imprecise_dtypes=True).then_inc(part_mod_set, 1)
                pool.wait_ge(part_mod_set, q + 1)
            pool.wait_ge(zero_set, 1)
            pool.dma_start(h2buf[SEQ:ROWS, :], zeros[:, :]).then_inc(zeros_stored, 16)
            pool.dma_start(acc[SEQ:ROWS, :], zeros[:, :]).then_inc(zeros_stored, 16)

            pool.wait_ge(branches_used, 1)
            pool.wait_ge(merged, KD)
            for q in range(3):
                rows = slice(32 * q, 32 * q + 32)
                pool.dma_start(bias32[rows, 0:2 * FF], b_gate_up[0]).then_inc(bias_in, 16)
                pool.dma_start(bias32[rows, 2 * FF:3 * FF], b_down[0]).then_inc(bias_in, 16)
            pool.wait_ge(bias_in, 96)
            chain = [2]

            def link(ins):
                chain[0] += 1
                ins.then_inc(pool_step, 1)
                pool.wait_ge(pool_step, chain[0])

            part1, part2 = slice(32, 64), slice(64, 96)
            link(g.memset(bias_tab[96:128, :], 0.0))
            link(g.tensor_copy(bias_tab[0:96, :], bias32[0:96, :]))
            for rows in (part1, part2):
                link(g.tensor_tensor(bias32[rows, :], bias32[rows, :], bias_tab[rows, :], ALU.subtract))
                link(g.tensor_copy(bias_tab[rows, :], bias32[rows, :]))
            link(g.tensor_tensor(bias32[part2, :], bias32[part2, :], bias_tab[part2, :], ALU.subtract))
            g.tensor_copy(bias_tab[part2, :], bias32[part2, :]).then_inc(bias_ready, 1)
            pool.wait_ge(bias_ready, 1)

            pool.wait_ge(rows_stored, 2 * NT * 16)
            pool.wait_ge(zeros_stored, 32)
            pool.wait_ge(items_ready, 1)
            items = pool.value_load(items_i[0:1, 0:1], min_val=E, max_val=E * PASSES)

            def gather():
                g.indirect_dma_start(out=xg, out_offset=None, in_=h2buf,
                                     in_offset=bass.IndirectOffsetOnAxis(ap=idx_g[:, 0:1], axis=0)
                                     ).then_inc(gathered, 16)

            pool.wait_ge(idx_ready, 1)
            gather()
            g.tensor_copy(idx_s[:, :], idx_g[:, :]).then_inc(idx_kept, 1)
            with pool.Fori(0, items) as i:
                pool.wait_ge(idx_ready, i + 2)
                pool.wait_ge(xt_ps, i + 1)
                pool.sem_inc(pool_past, 1)
                gather()
                pool.wait_ge(y_ready, 2 * i + 3)
                pool.wait_ge(idx_kept, i + 1)
                pool.sem_inc(pool_past, 1)
                g.indirect_dma_start(out=acc, out_offset=bass.IndirectOffsetOnAxis(ap=idx_s[:, 0:1], axis=0),
                                     in_=ysb, in_offset=None, compute_op=ALU.add).then_inc(scattered, 16)
                pool.wait_ge(scattered, 16 * i + 16)
                pool.sem_inc(pool_past, 1)
                g.tensor_copy(idx_s[:, :], idx_g[:, :]).then_inc(idx_kept, 1)

        @block.scalar
        def _(act):
            a = nc.scalar
            act.dma_start(g16[0:8, :], g_mix.rearrange("l (k p) -> (l k) p", p=128)).then_inc(g_mix_in, 16)
            act.wait_ge(eps_set, 1)
            a.activation(warm[:, :], eps[:, :], ACT.Sqrt)
            for c in range(NT):
                act.wait_ge(x_in[c], 16)
                a.activation(xn[:, c, :], xs[:, c, :], ACT.Square, accum_out=ss[:, c:c + 1]).then_inc(sq_done, 1)
                act.wait_ge(sq_done, c + 1)
                a.activation(ss[:, c:c + 1], ss[:, c:c + 1], ACT.Sqrt, bias=eps[:, 0:1],
                             scale=1.0 / D).then_inc(rt_done, 1)
            act.dma_start(rp, rope.rearrange("(c p) t n -> p c t n", p=128)).then_inc(consts_in, 16)
            act.dma_start(gains[:, 0, :], qa_norm[0:1, :].to_broadcast([128, HD])).then_inc(consts_in, 16)
            act.dma_start(gains[:, 1, :], ka_norm[0:1, :].to_broadcast([128, HD])).then_inc(consts_in, 16)
            act.dma_start(sink[:, :], sink_b[0:1, :].to_broadcast([128, 8])).then_inc(consts_in, 16)
            act.dma_start(brt[:, :], b_router[0:1, :].to_broadcast([128, E])).then_inc(consts_in, 16)

            def in_split_hi(n):
                if n >= IN_CHUNKS:
                    return
                act.wait_ge(chunk_in[n % NIN], 16 * (n // NIN + 1))
                if n >= NIN_SPLIT:
                    act.wait_ge(in_used, n - NIN_SPLIT + 1)
                a.activation(split[:, n % NIN_SPLIT, 0, :], raw[:, n % NIN, :], ACT.Copy).then_inc(in_hi, 1)

            in_split_hi(0)
            act.wait_ge(gcol_ready, 1)
            for k in range(KD):
                act.wait_ge(hT_ps, k + 1)
                a.activation(hT[:, 0, k, :], ps[:, k, :], ACT.Copy, scale=gcol[:, k:k + 1]).then_inc(hT_hi, 1)
                if k % 4 == 3:
                    in_split_hi(1 + k // 4)

            def project_out(n):
                grp, c = n // NT, n % NT
                act.wait_ge(proj_ps, n + 1)
                src = ps[:, n % 4, :]
                if grp >= 3:
                    a.activation(gT[:, n - 12, :], src, ACT.Sigmoid).then_inc(proj_out, 1)
                    return
                if grp == 0:
                    a.activation(qk[:, c, 0:512], src, ACT.Copy).then_inc(proj_out, 1)
                    return
                if grp == 1:
                    kv, q, q_at, k_at, v_at = src[:, 0:256], src[:, 256:512], 768, 512, 0
                else:
                    kv, q, q_at, k_at, v_at = src[:, 256:512], src[:, 0:256], 1024, 1280, 128
                a.activation(qk[:, c, q_at:q_at + 256], q, ACT.Copy)
                k_dst = qk[:, c, k_at:k_at + 256].rearrange("p (h two n) -> p h two n", h=2, two=2)
                k_src = kv[:, 0:128].rearrange("p (h n) -> p h n", h=2)
                a.activation(k_dst[:, :, 0, :], k_src, ACT.Copy)
                a.activation(k_dst[:, :, 1, :], k_src, ACT.Copy)
                a.activation(v_sb[:, c, v_at:v_at + 128], kv[:, 128:256], ACT.Copy).then_inc(proj_out, 1)

            act.wait_ge(xn_ready, NT)
            act.wait_ge(hT_ps, KD)
            act.wait_ge(zeros_stored, 32)
            for grp in range(7):
                if grp:
                    in_split_hi(2 * grp + 2)
                project_out(4 * grp)
                if grp >= 3:
                    c = grp - 3
                    act.wait_ge(hs_ready, c + 1)
                    a.activation(hs[:, c, :], hs[:, c, :], ACT.Sqrt, bias=eps[:, 0:1],
                                 scale=1.0 / HD).then_inc(hrt_done, 1)
                project_out(4 * grp + 1)
                project_out(4 * grp + 2)
                in_split_hi(2 * grp + 3)
                project_out(4 * grp + 3)
            act.wait_ge(in_used, IN_CHUNKS)
            act.dma_start(wr[:, :, :], kp(w_router[0])).then_inc(late_in, 16)
            act.dma_start(gffn[:, :], g_ffn[0:1, :].to_broadcast([128, D])).then_inc(late_in, 16)
            for n in range(1, 12, 2):
                act.wait_ge(qT_ps, n + 1)
                c, t = n // 3, n % 3
                a.activation(qT[:, 4 * t:4 * t + 4, c * 128:(c + 1) * 128],
                             ps[:, 4 + t, :].rearrange("p (t n) -> p t n", n=128), ACT.Copy).then_inc(qT_a, 1)

            def exps(j):
                w = SEQ if j < 8 else WW
                act.wait_ge(negm_ready, j + 1)
                if j >= 2:
                    act.wait_ge(pT_ps, 4 * (j - 1))
                for n in range(4):
                    a.activation(probs[:, j % 2, n, 0:w], ps[:, n, 0:w], ACT.Exp, bias=negm[:, j % 2, n:n + 1],
                                 scale=SCALE, accum_out=psum_p[:, j % 2, n:n + 1]).then_inc(exps_done, 1)
                if j >= 8:
                    a.activation(esink[:, j % 2, :], negm[:, j % 2, :], ACT.Exp,
                                 bias=sink[:, j - 8:j - 7]).then_inc(esink_done, 1)

            exps(0)
            for j in range(JOBS):
                for kb in range(2):
                    act.wait_ge(pT_ps, 4 * j + kb + 1)
                    if j:
                        act.wait_ge(pv_ps, j)
                    q0, q1 = (0, NT) if j < 8 else (window(kb)[0], window(kb)[-1] + 1)
                    a.activation(pT[:, kb, q0 * 128:q1 * 128], ps[:, 4 + (4 * j + kb) % 3, q0 * 128:q1 * 128],
                                 ACT.Copy).then_inc(pT_a, 1)
                if j + 1 < JOBS:
                    exps(j + 1)

            def h2T_half(c):
                act.wait_ge(h2T_ps, c + 1)
                if c >= 2:
                    act.wait_ge(logits_ps, c - 1)
                a.activation(h2T[:, c % 2, 0:4, :], ps[:, 0, :].rearrange("p (k n) -> p k n", n=128),
                             ACT.Copy).then_inc(h2T_a, 1)

            act_v = acc[0:SEQ, :].rearrange("(c p) n -> c p n", p=128)
            h2_v = h2buf[0:SEQ, :].rearrange("(c p) n -> c p n", p=128)
            for c in range(NT):
                act.wait_ge(x1_ready, 2 * c + 2)
                act.dma_start(act_v[c], xs[:, c, :]).then_inc(rows_stored, 16)
                a.activation(xn[:, c, :], xs[:, c, :], ACT.Square, accum_out=ss[:, c:c + 1]).then_inc(sq2_done, 1)
                act.wait_ge(sq2_done, c + 1)
                a.activation(ss[:, c:c + 1], ss[:, c:c + 1], ACT.Sqrt, bias=eps[:, 0:1],
                             scale=1.0 / D).then_inc(rt2_done, 1)
                if c == NT - 1:
                    h2T_half(c - 1)
                act.wait_ge(xn2_ready, c + 1)
                act.dma_start(h2_v[c], xn[:, c, :]).then_inc(rows_stored, 16)
                if c != NT - 2:
                    h2T_half(c)
            for c in range(NT):
                act.wait_ge(lg_ready, c + 1)
                a.activation(ex[:, c, :], lg[:, c, :], ACT.Exp, bias=negl[:, c:c + 1]).then_inc(ex_done, 1)

            def ex_split_hi(i, s):
                act.wait_ge(expert_in[s], (i + 1) * 16)
                act.wait_ge(ex_used, i * NCH + s + 1)
                a.activation(split[:, s % NSPLIT, 0, :], raw_slot(i, s), ACT.Copy).then_inc(ex_hi, 1)

            ex_split_hi(0, 0)
            ex_split_hi(0, 1)
            act.wait_ge(logits_ps, NT)
            ex_split_hi(0, 2)
            act.wait_ge(bias_ready, 1)
            ex_split_hi(0, 3)
            ex_split_hi(0, 4)
            act.wait_ge(rows_stored, 2 * NT * 16)
            ex_split_hi(0, 5)

            def rows_hi(n):
                act.wait_ge(xt_ps, n)
                for t in range(2):
                    last = a.activation(XT[:, 0, 4 * t:4 * t + 4, :],
                                        ps[:, t, 0:4 * CAP].rearrange("p (k n) -> p k n", n=CAP), ACT.Copy)
                last.then_inc(xt_hi, 1)

            def hidden_hi(half, n):
                act.wait_ge(hidT_ps, n)
                a.activation(hidT[:, 0, 4 * half:4 * half + 4, :],
                             ps[:, 6 + half, 0:4 * CAP].rearrange("p (k n) -> p k n", n=CAP),
                             ACT.Copy).then_inc(hidT_hi, 1)

            rows_hi(1)
            act.wait_ge(items_ready, 1)
            last_item = act.value_load(items_i[0:1, 1:2], min_val=E - 1, max_val=E * PASSES - 1)
            act.sem_inc(y_ready, 1)

            def act_item(i, nxt):
                a.activation(warm[:, :], eps[:, :], ACT.Sigmoid)
                for s in (6, 7, 8):
                    ex_split_hi(i, s)
                act.wait_ge(clamp_ready, 2 * i + 1)
                a.activation(sg, gc, ACT.Sigmoid, scale=1.702).then_inc(sig_done, 1)
                for s in (9, 10, 11):
                    ex_split_hi(i, s)
                hidden_hi(0, 2 * i + 2)
                if nxt:
                    ex_split_hi(i + 1, 0)
                act.wait_ge(clamp_ready, 2 * i + 2)
                a.activation(sg, gc, ACT.Sigmoid, scale=1.702).then_inc(sig_done, 1)
                if nxt:
                    ex_split_hi(i + 1, 1)
                    ex_split_hi(i + 1, 2)
                hidden_hi(1, 2 * i + 3)
                act.wait_ge(pair_ps, 2 * i + 2)
                rows_hi(i + 2)
                if nxt:
                    for s in (3, 4, 5):
                        ex_split_hi(i + 1, s)
                act.wait_ge(y_ps, i + 1)
                act.wait_ge(gate_ready, i + 1)
                act.wait_ge(idx_kept, i + 1)
                for t in range(2):
                    a.activation(ysb[:, t * 512:(t + 1) * 512], ps[0:CAP, 4 + t, :], ACT.Copy,
                                 scale=gate_c[:, 0:1]).then_inc(y_ready, 1)

            with act.Fori(0, last_item) as i:
                act_item(i, True)
            act_item(last_item, False)

            act.dma_start(gfin, g_final.rearrange("(l n) -> l n", l=1).to_broadcast([128, D])).then_inc(gfin_in, 16)
            for c in range(NT):
                act.wait_ge(acc_in[c], 16)
                a.activation(fin_sq[:, c, :], fin[:, c, :], ACT.Square, accum_out=ss[:, c:c + 1]).then_inc(fsq_done, 1)
                act.wait_ge(fsq_done, c + 1)
                a.activation(ss[:, c:c + 1], ss[:, c:c + 1], ACT.Sqrt, bias=eps[:, 0:1],
                             scale=1.0 / D).then_inc(frt_done, 1)

        @block.vector
        def _(dve):
            v = nc.vector
            steps = [0]

            def link(ins):
                steps[0] += 1
                ins.then_inc(dve_step, 1)
                dve.wait_ge(dve_step, steps[0])

            for c in range(NT):
                dve.wait_ge(rt_done, c + 1)
                link(v.reciprocal(rstd[:, c:c + 1], ss[:, c:c + 1]))
                v.tensor_scalar(xn[:, c, :], xs[:, c, :], rstd[:, c:c + 1], None, ALU.mult).then_inc(xn_ready, 1)
                if c == 0:
                    dve.wait_ge(gcol_ps, 1)
                    v.tensor_copy(gcol[:, :], ps[:, 7, 0:KD]).then_inc(gcol_ready, 1)
            dve.wait_ge(gcol_ready, 1)

            def in_split_lo(n):
                if n >= IN_CHUNKS:
                    return
                dve.wait_ge(in_hi, n + 1)
                v.tensor_tensor(split[:, n % NIN_SPLIT, 1, :], raw[:, n % NIN, :],
                                split[:, n % NIN_SPLIT, 0, :].bitcast(F32), ALU.subtract).then_inc(in_lo, 1)

            in_split_lo(0)
            for k in range(KD):
                dve.wait_ge(hT_hi, k + 1)
                v.scalar_tensor_tensor(out=hT[:, 1, k, :], in0=ps[:, k, :], scalar=gcol[:, k:k + 1],
                                       in1=hT[:, 0, k, :].bitcast(F32), op0=ALU.mult,
                                       op1=ALU.subtract).then_inc(hT_lo, 1)
                if k % 4 == 3:
                    in_split_lo(1 + k // 4)
            for n in range(NIN_SPLIT, 8):
                in_split_lo(n)
            dve.wait_ge(consts_in, 80)
            for c in range(NT):
                dve.wait_ge(proj_out, 8 + c + 1)
                in_split_lo(2 * c + 8)
                if c:
                    dve.wait_ge(rope_done, c)
                qa = qk[:, c, 0:768].rearrange("p (h n) -> p h n", n=HD)
                link(v.tensor_tensor(rt1, qk[:, c, 0:768], qk[:, c, 0:768], ALU.mult))
                v.tensor_reduce(hs[:, c, :], rt1.rearrange("p (h n) -> p h n", n=HD), AX.X,
                                ALU.add).then_inc(hs_ready, 1)
                dve.wait_ge(hrt_done, c + 1)
                link(v.reciprocal(hs[:, c, :], hs[:, c, :]))
                link(v.tensor_tensor(qa, qa, hs[:, c, :].unsqueeze(2).to_broadcast([128, 12, HD]), ALU.mult))
                v.tensor_tensor(qa[:, 0:8, :], qa[:, 0:8, :],
                                gains[:, 0:1, :].to_broadcast([128, 8, HD]), ALU.mult)
                link(v.tensor_tensor(qa[:, 8:12, :], qa[:, 8:12, :],
                                     gains[:, 1:2, :].to_broadcast([128, 4, HD]), ALU.mult))
                last = None
                for br in range(2):
                    h = qk[:, c, br * 768:(br + 1) * 768].rearrange("p (h two n) -> p h two n", two=2, n=32)
                    x1, x2 = h[:, :, 0, :], h[:, :, 1, :]
                    cos = rp[:, c, 2 * br:2 * br + 1, :].to_broadcast([128, 12, 32])
                    sin = rp[:, c, 2 * br + 1:2 * br + 2, :].to_broadcast([128, 12, 32])
                    t1 = rt1[:, br * 384:(br + 1) * 384].rearrange("p (h n) -> p h n", n=32)
                    t2 = rt2[:, br * 384:(br + 1) * 384].rearrange("p (h n) -> p h n", n=32)
                    v.tensor_tensor(t1, x1, sin, ALU.mult)
                    link(v.tensor_tensor(t2, x2, sin, ALU.mult))
                    v.tensor_tensor(x1, x1, cos, ALU.mult)
                    link(v.tensor_tensor(x2, x2, cos, ALU.mult))
                    v.tensor_tensor(x1, x1, t2, ALU.subtract)
                    last = v.tensor_tensor(x2, x2, t1, ALU.add)
                last.then_inc(rope_done, 1)
                in_split_lo(2 * c + 9)
            for n in range(0, 12, 2):
                dve.wait_ge(qT_ps, n + 1)
                c, t = n // 3, n % 3
                v.tensor_copy(qT[:, 4 * t:4 * t + 4, c * 128:(c + 1) * 128],
                              ps[:, 4 + t, :].rearrange("p (t n) -> p t n", n=128)).then_inc(qT_d, 1)

            def row_max(j):
                w = SEQ if j < 8 else WW
                dve.wait_ge(scores_ps, j + 1)
                if j:
                    dve.wait_ge(negm_ready, j)
                link(v.reduce_max(mx[:, :], ps[:, 0:4, 0:w], AX.X))
                if j < 8:
                    v.tensor_scalar(negm[:, j % 2, :], mx[:, :], -SCALE, None, ALU.mult).then_inc(negm_ready, 1)
                else:
                    link(v.tensor_scalar(mx[:, :], mx[:, :], SCALE, sink[:, j - 8:j - 7], ALU.mult, ALU.max))
                    v.tensor_scalar(negm[:, j % 2, :], mx[:, :], -1.0, None, ALU.mult).then_inc(negm_ready, 1)

            def diagonals(j):
                dve.wait_ge(exps_done, 4 * j + 4)
                total = psum_p[:, j % 2, :]
                if j >= 8:
                    dve.wait_ge(esink_done, j - 7)
                    link(v.tensor_tensor(total, total, esink[:, j % 2, :], ALU.add))
                if j:
                    dve.wait_ge(diag_ready, j)
                link(v.reciprocal(rinv[:, :], total))
                if j:
                    dve.wait_ge(pT_ps, 4 * j)
                for n in range(4):
                    last = v.tensor_scalar(diag[:, n, :], ident[:, :], rinv[:, n:n + 1], None, ALU.mult)
                last.then_inc(diag_ready, 1)

            row_max(0)
            diagonals(0)
            for j in range(JOBS):
                if j + 1 < JOBS:
                    row_max(j + 1)
                for kb in range(2, 4):
                    dve.wait_ge(pT_ps, 4 * j + kb + 1)
                    if j:
                        dve.wait_ge(pv_ps, j)
                    q0, q1 = (0, NT) if j < 8 else (window(kb)[0], window(kb)[-1] + 1)
                    v.tensor_copy(pT[:, kb, q0 * 128:q1 * 128],
                                  ps[:, 4 + (4 * j + kb) % 3, q0 * 128:q1 * 128]).then_inc(pT_d, 1)
                if j + 1 < JOBS:
                    diagonals(j + 1)
                if j % 2:
                    dve.wait_ge(pv_ps, j + 1)
                    v.tensor_copy((oTa if j < 8 else oTb)[:, j // 2 % 4, :], ps[:, 7, :]).then_inc(oT_out, 1)

            for c in range(KD):
                dve.wait_ge(branch_ps, c + 1)
                b = (c % 2) * 2
                if c >= 2:
                    dve.wait_ge(merged, c - 1)
                v.tensor_tensor(mT[:, c, :], gT[:, c, :], ps[:, b, :], ALU.mult)
                link(v.tensor_tensor(mtmp[:, c % 2, :], gT[:, 8 + c, :], ps[:, b + 1, :], ALU.mult))
                v.tensor_tensor(mT[:, c, :], mT[:, c, :], mtmp[:, c % 2, :], ALU.add).then_inc(merged, 1)

            def residual(c):
                for t in range(2):
                    n = 2 * c + t
                    dve.wait_ge(wout_ps, n + 1)
                    half = xs[:, c, t * 512:(t + 1) * 512]
                    v.tensor_tensor(half, half, ps[:, 4 + n % 4, :], ALU.add).then_inc(x1_ready, 1)

            def norm(c):
                dve.wait_ge(rt2_done, c + 1)
                if c == 0:
                    dve.wait_ge(late_in, 32)
                link(v.reciprocal(rstd[:, c:c + 1], ss[:, c:c + 1]))
                v.scalar_tensor_tensor(out=xn[:, c, :], in0=xs[:, c, :], scalar=rstd[:, c:c + 1], in1=gffn[:, :],
                                       op0=ALU.mult, op1=ALU.mult).then_inc(xn2_ready, 1)

            def h2_out(c):
                dve.wait_ge(h2T_ps, c + 1)
                if c >= 2:
                    dve.wait_ge(logits_ps, c - 1)
                v.tensor_copy(h2T[:, c % 2, 4:8, :],
                              ps[:, 1, :].rearrange("p (k n) -> p k n", n=128)).then_inc(h2T_d, 1)

            def choose(c):
                dve.wait_ge(logits_ps, c + 1)
                link(v.tensor_tensor(lg[:, c, :], ps[:, 2, c * E:(c + 1) * E], brt[:, :], ALU.add))
                if c:
                    dve.wait_ge(mask_ready, c)
                link(v.max(m8[:, :], lg[:, c, :]))
                v.tensor_scalar(negl[:, c:c + 1], m8[:, 0:1], -1.0, None, ALU.mult).then_inc(lg_ready, 1)
                link(v.tensor_copy(m8x[:, 0:TOPK], m8[:, 0:TOPK]))
                link(v.match_replace(out=repl[:, :], in_to_replace=m8x[:, :], in_values=lg[:, c, :],
                                     imm_value=-3e38))
                v.tensor_scalar(mask[:, c, :], repl[:, :], -3e38, None, ALU.is_equal).then_inc(mask_ready, 1)

            def softmax():
                dve.wait_ge(ex_done, NT)
                dve.wait_ge(mask_ready, NT)
                link(v.tensor_tensor(ex[:, :, :], ex[:, :, :], mask[:, :, :], ALU.mult))
                link(v.tensor_reduce(gsum[:, :], ex[:, :, :], AX.X, ALU.add))
                link(v.reciprocal(gsum[:, :], gsum[:, :]))
                link(v.tensor_tensor(ex[:, :, :], ex[:, :, :], gsum[:, :].unsqueeze(2).to_broadcast([128, NT, E]),
                                     ALU.mult))
                for part in range(3, 6):
                    link(v.tensor_copy(feats[:, :, :, part], ex[:, :, :]))
                    if part < 5:
                        link(v.tensor_tensor(ex[:, :, :], ex[:, :, :], feats[:, :, :, part], ALU.subtract))

            def ex_split_lo(i, s):
                dve.wait_ge(ex_hi, i * NCH + s + 1)
                v.tensor_tensor(split[:, s % NSPLIT, 1, :], raw_slot(i, s), split[:, s % NSPLIT, 0, :].bitcast(F32),
                                ALU.subtract).then_inc(ex_lo, 1)

            link(v.memset(m8x[:, :], 3e38))
            residual(0)
            norm(0)
            residual(1)
            norm(1)
            h2_out(0)
            residual(2)
            norm(2)
            choose(0)
            h2_out(1)
            residual(3)
            h2_out(2)
            norm(3)
            choose(1)
            choose(2)
            h2_out(3)
            choose(3)
            dve.wait_ge(pos_ps, 1)
            link(v.scalar_tensor_tensor(out=posx[:, :, :], in0=ps[:, 3, 0:128].rearrange("p (c e) -> p c e", e=E),
                                        scalar=1024.0, in1=mask[:, :, :], op0=ALU.add, op1=ALU.mult))
            v.tensor_scalar(posx[:, :, :], posx[:, :, :], -1024.0, None, ALU.add).then_inc(route_ready, 1)
            link(v.reduce_max(cmax[:, :], ps[:, 3, 128:160], AX.X))
            link(v.tensor_scalar(over[:, 0:PASSES - 1], passoff[:, 1:PASSES], cmax[:, 0:1], None, ALU.is_lt))
            link(v.tensor_reduce(npass[:, :], over[:, 0:PASSES - 1], AX.X, ALU.add))
            link(v.tensor_scalar(npass[:, :], npass[:, :], 1.0, float(E), ALU.add, ALU.mult))
            v.tensor_scalar(items_i[:, 1:2], npass[:, :], -1.0, None, ALU.add)
            v.tensor_copy(items_i[:, 0:1], npass[:, :]).then_inc(items_ready, 1)
            dve.wait_ge(items_ready, 1)
            last_item = dve.value_load(items_i[0:1, 1:2], min_val=E - 1, max_val=E * PASSES - 1)
            dve.wait_ge(route_ready, 1)

            softmax()
            base = steps[0]

            def serve(i, n_link):
                e, b = i % E, i // E
                v.tensor_scalar(tgt[:, :], posx[:, :, bass.ds(e, 1)].rearrange("p c one -> p (c one)"),
                                passoff[:, bass.ds(b, 1)], None, ALU.subtract).then_inc(dve_step, 1)
                dve.wait_ge(dve_step, n_link)
                v.tensor_tensor(onehot, iota_cap[:, :].unsqueeze(1).to_broadcast([128, NT, CAP]),
                                tgt[:, :].unsqueeze(2).to_broadcast([128, NT, CAP]),
                                ALU.is_equal).then_inc(onehot_ready, 1)

            def index(n, n_link, n_ready=None):
                dve.wait_ge(idx_done, n)
                v.tensor_copy(f6[:, :], idx_ps).then_inc(dve_step, 1)
                dve.wait_ge(dve_step, n_link)
                if n_ready is not None:
                    dve.wait_ge(idx_ready, n_ready)
                v.tensor_reduce(s1[:, :], f6[:, 0:2], AX.X, ALU.add)
                v.tensor_tensor(s2[:, :], f6[:, 2:3], idle_neg[0:CAP, :], ALU.mult).then_inc(dve_step, 1)
                dve.wait_ge(dve_step, n_link + 1)
                v.scalar_tensor_tensor(out=idx_g[:, :], in0=s2[:, :], scalar=idle_row[0:CAP, 0:1], in1=s1[:, :],
                                       op0=ALU.add, op1=ALU.add).then_inc(idx_ready, 1)

            def rows_lo(n):
                dve.wait_ge(xt_hi, n)
                for t in range(2):
                    last = v.tensor_tensor(XT[:, 1, 4 * t:4 * t + 4, :],
                                           ps[:, t, 0:4 * CAP].rearrange("p (k n) -> p k n", n=CAP),
                                           XT[:, 0, 4 * t:4 * t + 4, :].bitcast(F32), ALU.subtract)
                last.then_inc(xt_lo, 1)

            def hidden_lo(half, n):
                dve.wait_ge(hidT_hi, n)
                v.tensor_tensor(hidT[:, 1, 4 * half:4 * half + 4, :],
                                ps[:, 6 + half, 0:4 * CAP].rearrange("p (k n) -> p k n", n=CAP),
                                hidT[:, 0, 4 * half:4 * half + 4, :].bitcast(F32),
                                ALU.subtract).then_inc(hidT_lo, 1)

            serve(0, base + 1)
            index(1, base + 2)
            for s in range(5):
                ex_split_lo(0, s)
            rows_lo(1)
            ex_split_lo(0, 5)
            PER = 7
            dve.sem_inc(hid_ready, 1)
            dve.sem_inc(hidT_lo, 1)

            def dve_item(i, nxt):
                at = i * PER + base + 3
                dve.wait_ge(idx_done, i + 1)
                serve(i + 1, at + 1)
                e = i % E
                dve.wait_ge(down_begun, i + 1)
                v.tensor_scalar(sel[:, :], part_mod[:, :], erow[:, bass.ds(e, 1)], None,
                                ALU.is_equal).then_inc(sel_ready, 1)
                ex_split_lo(i, 6)
                dve.wait_ge(y_ready, 2 * i + 1)
                v.tensor_reduce(gate_c[:, :], f6[:, 3:6], AX.X, ALU.add).then_inc(gate_ready, 1)
                for s in (7, 8):
                    ex_split_lo(i, s)
                for half in range(2):
                    b = 2 * half
                    dve.wait_ge(pair_ps, 2 * i + half + 1)
                    dve.wait_ge(hid_ready, 2 * i + half + 1)
                    v.tensor_scalar(gc, ps[0:CAP, b, :], 7.0, None, ALU.min).then_inc(clamp_ready, 1)
                    v.tensor_scalar(uc, ps[0:CAP, b + 1, :], 7.0, -7.0, ALU.min, ALU.max).then_inc(dve_step, 1)
                    dve.wait_ge(dve_step, at + (2 if half == 0 else 6))
                    dve.wait_ge(clamp_ready, 2 * i + half + 1)
                    v.scalar_tensor_tensor(out=uc, in0=uc, scalar=1.0, in1=gc, op0=ALU.add,
                                           op1=ALU.mult).then_inc(dve_step, 1)
                    dve.wait_ge(dve_step, at + (3 if half == 0 else 7))
                    dve.wait_ge(sig_done, 2 * i + half + 1)
                    if half == 0:
                        dve.wait_ge(hidT_ps, 2 * i + 1)
                    v.tensor_tensor(hid[:, half * 512:(half + 1) * 512], uc, sg, ALU.mult).then_inc(hid_ready, 1)
                    if half == 0:
                        dve.wait_ge(idx_kept, i + 1)
                        dve.wait_ge(gate_ready, i + 1)
                        index(i + 2, at + 4, i + 1)
                        ex_split_lo(i, 9)
                        ex_split_lo(i, 10)
                        hidden_lo(0, 2 * i + 1)
                        ex_split_lo(i, 11)
                if nxt:
                    ex_split_lo(i + 1, 0)
                    ex_split_lo(i + 1, 1)
                hidden_lo(1, 2 * i + 2)
                if nxt:
                    ex_split_lo(i + 1, 2)
                rows_lo(i + 2)
                if nxt:
                    for s in (3, 4, 5):
                        ex_split_lo(i + 1, s)

            with dve.Fori(0, last_item) as i:
                dve_item(i, True)
            dve_item(last_item, False)

            dve.wait_ge(gfin_in, 16)
            links_done = last_item * PER + PER + base + 3
            for c in range(NT):
                dve.wait_ge(frt_done, c + 1)
                v.reciprocal(rstd[:, c:c + 1], ss[:, c:c + 1]).then_inc(dve_step, 1)
                dve.wait_ge(dve_step, links_done + c + 1)
                v.scalar_tensor_tensor(out=fin[:, c, :], in0=fin[:, c, :], scalar=rstd[:, c:c + 1], in1=gfin,
                                       op0=ALU.mult, op1=ALU.mult).then_inc(out_ready, 1)

        @block.tensor
        def _(pe):
            t_ = nc.tensor
            mm = t_.matmul

            def mm_split(dst, lhsT, rhs, start, stop):
                mm(dst, lhsT(0), rhs(0), start=start, stop=False)
                mm(dst, lhsT(0), rhs(1), start=False, stop=False)
                return mm(dst, lhsT(1), rhs(0), start=False, stop=stop)

            pe.wait_ge(ident_set, 1)
            pe.wait_ge(g_mix_in, 16)
            t_.transpose(ps[:, 7, 0:KD], g16[0:KD, :], ident[0:KD, 0:KD]).then_inc(gcol_ps, 1)
            pe.wait_ge(gcol_ready, 1)
            for c in range(NT):
                pe.wait_ge(xn_ready, c + 1)
                for k in range(KD):
                    last = t_.transpose(ps[:, k, c * 128:(c + 1) * 128], xn[:, c, k * 128:(k + 1) * 128], ident[:, :])
                    if c == NT - 1:
                        last.then_inc(hT_ps, 1)
            for grp in range(7):
                for c in range(4):
                    n = 4 * grp + c
                    if n >= 4:
                        pe.wait_ge(proj_out, n - 3)
                    for k in range(KD):
                        if n == 0:
                            pe.wait_ge(hT_lo, k + 1)
                        elif n < 4 and k == 0:
                            pe.wait_ge(hT_lo, KD)
                        m = 2 * grp + k // 4
                        if c == 0 and k % 4 == 0:
                            pe.wait_ge(in_lo, m + 1)

                        def w(part, lo=0, hi=512):
                            at = (k % 4) * 512
                            return split[:, m % NIN_SPLIT, part, at + lo:at + hi]

                        if grp < 3:
                            last = mm_split(ps[:, n % 4, :], lambda p: hT[:, p, k, c * 128:(c + 1) * 128], w,
                                            start=(k == 0), stop=(k == KD - 1))
                        else:
                            last = mm_split(ps[:, n % 4, :], lambda p: w(p, c * 128, (c + 1) * 128),
                                            lambda p: hT[:, p, k, :], start=(k == 0), stop=(k == KD - 1))
                        if c == 3 and k == 3:
                            last.then_inc(in_used, 1)
                    last.then_inc(proj_ps, 1)
                pe.wait_ge(proj_ps, 4 * grp + 4)
                pe.sem_inc(in_used, 1)
            for n in range(12):
                c, t = n // 3, n % 3
                if t == 0:
                    pe.wait_ge(rope_done, c + 1)
                if n >= 3:
                    pe.wait_ge(qT_a if n % 2 == 0 else qT_d, (n - 3) // 2 + 1)
                for u in range(4):
                    col = (4 * t + u) * 128
                    last = t_.transpose(ps[:, 4 + t, u * 128:(u + 1) * 128], qk[:, c, col:col + 128], ident[:, :])
                last.then_inc(qT_ps, 1)
            pe.wait_ge(qT_a, 6)
            pe.wait_ge(qT_d, 6)
            pe.wait_ge(proj_out, 28)

            pe.wait_ge(pool_consts, 1)
            def scores(j):
                br, h = j // 8, j % 8
                if j:
                    pe.wait_ge(exps_done, 4 * j)
                r = slice(64 * (h % 2), 64 * (h % 2) + 64)
                q, k = qT[r, 6 * br + h // 2, :], qT[r, 6 * br + 4 + h // 4, :]
                for n in range(NT):
                    qn = q[:, n * 128:(n + 1) * 128]
                    if br == 0:
                        last = mm(ps[:, n, :], qn, k, start=True, stop=True)
                        continue
                    w = window(n)
                    c0 = (w[0] - n + 1) * 128
                    mm(ps[:, n, c0:c0 + 128 * len(w)], qn, k[:, w[0] * 128:(w[-1] + 1) * 128], start=True, stop=False)
                    mm(ps[:, n, 0:128], identb[:, :], (mask_lo if n else mask_all)[:, :], start=False, stop=False)
                    last = mm(ps[:, n, 256:384], identb[:, :], (mask_hi if n < NT - 1 else mask_all)[:, :],
                              start=False, stop=True)
                last.then_inc(scores_ps, 1)

            def values(j):
                br, h = j // 8, j % 8
                pe.wait_ge(diag_ready, j + 1)
                for kb in range(NT):
                    m = 4 * j + kb
                    old = m - 3
                    if old >= 0:
                        oj, okb = old // 4, old % 4
                        if okb < 2:
                            pe.wait_ge(pT_a, 2 * oj + okb + 1)
                        else:
                            pe.wait_ge(pT_d, 2 * oj + okb - 1)
                    for n in (range(NT) if br == 0 else window(kb)):
                        c0 = kb * 128 if br == 0 else (kb - n + 1) * 128
                        last = mm(ps[:, 4 + m % 3, n * 128:(n + 1) * 128], probs[:, j % 2, n, c0:c0 + 128],
                                  diag[:, n, :], start=True, stop=True)
                    last.then_inc(pT_ps, 1)
                vc = br * 128 + (h // 4) * 64
                o = ps[64 * (h % 2):64 * (h % 2) + 64, 7, :]
                if h % 2 == 0 and j:
                    pe.wait_ge(oT_out, j // 2)
                if br == 0:
                    for kb in range(NT):
                        if kb < 2:
                            pe.wait_ge(pT_a, 2 * j + kb + 1)
                        else:
                            pe.wait_ge(pT_d, 2 * j + kb - 1)
                        last = mm(o, v_sb[:, kb, vc:vc + 64], pT[:, kb, :], start=(kb == 0), stop=(kb == NT - 1))
                else:
                    pe.wait_ge(pT_a, 2 * j + 2)
                    for n in range(NT):
                        pe.wait_ge(pT_d, 2 * j + (1 if n < 2 else 2))
                        w = window(n)
                        for kb in w:
                            last = mm(o[:, n * 128:(n + 1) * 128], v_sb[:, kb, vc:vc + 64],
                                      pT[:, kb, n * 128:(n + 1) * 128], start=(kb == w[0]), stop=(kb == w[-1]))
                last.then_inc(pv_ps, 1)

            scores(0)
            for j in range(JOBS):
                if j + 1 < JOBS:
                    scores(j + 1)
                values(j)

            pe.wait_ge(oT_out, 8)
            for n in range(IN_CHUNKS, CHUNKS):
                pe.wait_ge(chunk_in[n % NIN], 16 * (n // NIN + 1))
            for c in range(KD):
                if c >= 2:
                    pe.wait_ge(merged, c - 1)
                for br in range(2):
                    for k in range(4):
                        w = blocks(raw[:, (IN_CHUNKS + 2 * br + k // 2) % NIN, :], D)[:, k % 2, c * 128:(c + 1) * 128]
                        last = mm(ps[:, (c % 2) * 2 + br, :], w, (oTa, oTb)[br][:, k, :],
                                  start=(k == 0), stop=(k == 3))
                last.then_inc(branch_ps, 1)
            pe.wait_ge(branch_ps, KD)
            pe.sem_inc(branches_used, 1)
            pe.wait_ge(merged, KD)
            for s in range(4):
                pe.wait_ge(wo_in[s], 16)

            def out_proj(c):
                for t in range(2):
                    n = 2 * c + t
                    if n >= 4:
                        pe.wait_ge(x1_ready, n - 3)
                    for k in range(KD):
                        last = mm(ps[:, 4 + n % 4, :], mT[:, k, c * 128:(c + 1) * 128],
                                  blocks(wo[:, k // 2, :], D)[:, k % 2, t * 512:(t + 1) * 512],
                                  start=(k == 0), stop=(k == KD - 1))
                    last.then_inc(wout_ps, 1)

            def h2_transpose(c):
                pe.wait_ge(xn2_ready, c + 1)
                if c:
                    pe.wait_ge(h2T_a, c)
                    pe.wait_ge(h2T_d, c)
                for k in range(KD):
                    last = t_.transpose(ps[:, k // 4, (k % 4) * 128:(k % 4 + 1) * 128],
                                        xn[:, c, k * 128:(k + 1) * 128], ident[:, :])
                last.then_inc(h2T_ps, 1)

            def router(c):
                pe.wait_ge(h2T_a, c + 1)
                pe.wait_ge(h2T_d, c + 1)
                if c:
                    pe.wait_ge(lg_ready, c)
                for k in range(KD):
                    last = mm(ps[:, 2, c * E:(c + 1) * E], h2T[:, c % 2, k, :], wr[:, k, :],
                              start=(k == 0), stop=(k == KD - 1))
                last.then_inc(logits_ps, 1)

            out_proj(0)
            out_proj(1)
            h2_transpose(0)
            out_proj(2)
            router(0)
            h2_transpose(1)
            out_proj(3)
            pe.wait_ge(wout_ps, 2 * NT)
            pe.sem_inc(ex_used, NSPLIT)
            h2_transpose(2)
            router(1)
            router(2)
            h2_transpose(3)
            router(3)
            for c in range(NT):
                pe.wait_ge(mask_ready, c + 1)
                for d in range(c + 1):
                    mm(ps[:, 3, c * E:(c + 1) * E], (tri if d == c else onesb)[:, :], mask[:, d, :],
                       start=(d == 0), stop=(d == c))
            for d in range(NT):
                last = mm(ps[:, 3, 128:128 + E], onesb[:, :], mask[:, d, :], start=(d == 0), stop=(d == NT - 1))
            last.then_inc(pos_ps, 1)

            def slots(i, n):
                pe.wait_ge(onehot_ready, n)
                pe.wait_ge(hidT_lo, 2 * i - 1)
                for c in range(NT):
                    last = mm(idx_ps, onehot[:, c, :],
                              feats[:, c, bass.ds(i % E, 1), :].rearrange("p one f -> p (one f)"),
                              start=(c == 0), stop=(c == NT - 1))
                last.then_inc(idx_done, 1)

            def rows_in(n):
                pe.wait_ge(gathered, n * 16)
                for k in range(KD):
                    last = t_.transpose(ps[:, k // 4, (k % 4) * CAP:(k % 4 + 1) * CAP],
                                        xg[:, (k // 2) * 256 + k % 2:(k // 2 + 1) * 256:2], ident[0:CAP, 0:CAP])
                last.then_inc(xt_ps, 1)

            pe.wait_ge(items_ready, 1)
            items = pe.value_load(items_i[0:1, 0:1], min_val=E, max_val=E * PASSES)
            pe.wait_ge(onehot_ready, 1)
            for c in range(NT):
                last = mm(idx_ps, onehot[:, c, :], feats[:, c, 0, :], start=(c == 0), stop=(c == NT - 1))
            last.then_inc(idx_done, 1)
            rows_in(1)
            pe.wait_ge(bias_ready, 1)
            pe.sem_inc(down_begun, 1)
            pe.sem_inc(hidT_ps, 1)
            with pe.Fori(0, items) as i:
                def hidden_T(half):
                    pe.wait_ge(hid_ready, 2 * i + half + 2)
                    if half:
                        pe.wait_ge(idx_ready, i + 2)
                    for k in range(4):
                        last = t_.transpose(ps[:, 6 + half, k * CAP:(k + 1) * CAP],
                                            hid[:, half * 512 + (k // 2) * 256 + k % 2:
                                                half * 512 + (k // 2 + 1) * 256:2],
                                            ident[0:CAP, 0:CAP])
                    last.then_inc(hidT_ps, 1)

                pe.wait_ge(xt_lo, i + 1)
                for half in range(2):
                    b = 2 * half
                    if half:
                        slots(i + 1, i + 2)
                        pe.wait_ge(hid_ready, 2 * i + 1)
                    for s in range(4 * half, 4 * half + 4):
                        pe.wait_ge(ex_lo, i * NCH + s + 1)
                        for k in range(2):
                            for t in range(2):
                                last = mm_split(ps[0:CAP, b + t, :], lambda p: XT[:, p, 2 * (s % 4) + k, :],
                                                lambda p: expert_w(s, p, k, t),
                                                start=(s % 4 == 0 and k == 0), stop=False)
                        last.then_inc(ex_used, 1)
                        if s == 6:
                            hidden_T(0)
                    pe.wait_ge(sel_ready, i + 1)
                    for t in range(2):
                        col = t * FF + half * 512
                        last = mm(ps[0:CAP, b + t, :], sel[:, :], bias_tab[:, col:col + 512], start=False, stop=True)
                    last.then_inc(pair_ps, 1)

                pe.wait_ge(y_ready, 2 * i + 1)
                for t in range(2):
                    col = 2 * FF + t * 512
                    last = mm(ps[0:CAP, 4 + t, :], sel[:, :], bias_tab[:, col:col + 512], start=True, stop=False)
                last.then_inc(down_begun, 1)
                for half in range(2):
                    if half:
                        hidden_T(1)
                        rows_in(i + 2)
                    pe.wait_ge(hidT_lo, 2 * i + half + 2)
                    for s in range(8 + 2 * half, 10 + 2 * half):
                        pe.wait_ge(ex_lo, i * NCH + s + 1)
                        for k in range(2):
                            for t in range(2):
                                last = mm_split(ps[0:CAP, 4 + t, :], lambda p: hidT[:, p, 2 * (s - 8) + k, :],
                                                lambda p: expert_w(s, p, k, t),
                                                start=False, stop=(s == 11 and k == 1))
                        last.then_inc(ex_used, 1)
                pe.wait_ge(ex_used, (i + 1) * NCH + NSPLIT)
                pe.sem_inc(y_ps, 1)


_INS = ['x', 'g_mix', 'w_in', 'qa_norm', 'ka_norm', 'sink_b', 'w_branch_a', 'w_branch_b', 'w_out', 'g_ffn', 'w_router',
        'b_router', 'w_gate_up', 'b_gate_up', 'w_down', 'b_down', 'g_final']


def rope_tables():
    grid = 64
    t = np.arange(SEQ)
    inv_ax = np.float32(10000.0) ** (-np.arange(0, HD // 2, 2, dtype=np.float32) / np.float32(HD // 2))
    inv_1d = np.float32(10000.0) ** (-np.arange(0, HD, 2, dtype=np.float32) / np.float32(HD))
    row, col = (t // grid).astype(np.float32), (t % grid).astype(np.float32)
    ax = np.concatenate([row[:, None] * inv_ax, col[:, None] * inv_ax], axis=-1).astype(np.float32)
    d1 = (t.astype(np.float32)[:, None] * inv_1d).astype(np.float32)
    return np.stack([np.cos(ax), np.sin(ax), np.cos(d1), np.sin(d1)], axis=1).astype(np.float32)


def kernel(**inputs):
    import concourse.bacc as _bacc
    from concourse.bass_utils import run_bass_kernel_spmd as _run

    nc = _bacc.Bacc("TRN2", target_bir_lowering=False, num_devices=1)
    f32 = mybir.dt.float32
    arrays, args = {}, []
    for name in _INS:
        a = np.ascontiguousarray(inputs[name])
        arrays[f"in_{name}"] = a
        args.append(nc.dram_tensor(f"in_{name}", a.shape, mybir.dt.from_np(a.dtype), kind="ExternalInput").ap())
    tables = rope_tables()
    arrays["rope_tables"] = tables
    args.append(nc.dram_tensor("rope_tables", tables.shape, f32, kind="ExternalInput").ap())
    args.append(nc.dram_tensor("h2_rows", (SEQ + CAP, D), f32, kind="Internal").ap())
    args.append(nc.dram_tensor("sum_rows", (SEQ + CAP, D), f32, kind="Internal").ap())
    args.append(nc.dram_tensor("out", (1, SEQ, D), f32, kind="ExternalOutput").ap())
    encoder_block(nc, *args)
    r = _run(nc, [arrays], core_ids=[0])
    return r.results[0]["out"]
```

```python
import numpy as np
import concourse.bass as bass
from concourse import mybir
from contextlib import ExitStack

SEQ, D, HD = 512, 1024, 64
NT, KD = SEQ // 128, D // 128
E, FF, TOPK = 32, 1024, 4
CAP = 96
PASSES = -(-SEQ // CAP)
EPS = 1e-6
SLOT = 2048
NRAW = 8
NSPLIT = 6
NIN, NIN_SPLIT = 4, 3
NCH = 12


def encoder_block(nc, x, g_mix, w_in, qa_norm, ka_norm, sink_b, w_branch_a, w_branch_b, w_out, g_ffn, w_router,
                  b_router, w_gate_up, b_gate_up, w_down, b_down, g_final, rope, h2buf, acc, bias_parts, out):
    F32, BF16, I32, F32R = mybir.dt.float32, mybir.dt.bfloat16, mybir.dt.int32, mybir.dt.float32r
    ALU, ACT, AX = mybir.AluOpType, mybir.ActivationFunctionType, mybir.AxisListType
    NEG = -1e30
    ROWS = SEQ + CAP
    JOBS = 16
    SCALE = HD ** -0.5

    ctx = ExitStack()
    with ctx:
        def sb(name, shape, dt=F32):
            return ctx.enter_context(nc.sbuf_tensor(name, shape, dt))

        def sem(name):
            return ctx.enter_context(nc.semaphore(name))

        ARENA = (nc.sbuf_usable_end - 196 * 1024) // 32 * 32

        def at(name, kib, shape, dt=F32):
            return nc.alloc_sbuf_tensor_at(name, shape, dt, offset=ARENA + int(kib * 1024))

        raw = at("raw", 0, [128, NRAW, SLOT])
        gT = at("gates_T", 32, [128, 16, SEQ])
        zeros = at("zeros", 32, [CAP, D])
        split = at("split", 64, [128, NSPLIT, 2, SLOT], F32R)
        g16 = at("g16", 96, [16, 128])
        diag = at("diag", 96, [128, 4, 128])
        wr = at("w_router", 98, [128, KD, E])
        gffn = at("g_ffn_rows", 100, [128, D])
        hT = at("hT", 112, [128, 2, KD, SEQ], F32R)
        qT = at("qT", 112, [128, 12, SEQ])
        xs = at("xs", 144, [128, NT, D])
        xn = at("xn", 160, [128, NT, D])
        qk = at("qk", 160, [128, NT, 1536])
        probs = at("probs", 160, [128, 2, 4, 512])
        v_sb = at("v", 184, [128, NT, 256])
        rt1_t = at("rt1", 188, [128, 768])
        rt2_t = at("rt2", 191, [128, 768])
        pT = at("pT", 188, [128, 4, SEQ])
        br_hi = at("branch_hi", 64, [128, 4, SLOT], F32R)
        br_lo = at("branch_lo", 0, [128, 4, SLOT], F32R)
        oTa, oTa_lo = at("oT_a", 136, [128, 4, SEQ]), at("oT_a_lo", 136, [128, 4, SEQ], F32R)
        oTa_hi = at("oT_a_hi", 112, [128, 4, SEQ], F32R)
        oTb, oTb_lo = at("oT_b", 176, [128, 4, SEQ]), at("oT_b_lo", 176, [128, 4, SEQ], F32R)
        oTb_hi = at("oT_b_hi", 104, [128, 4, SEQ], F32R)
        mT, mT_lo = at("merged_T", 160, [128, KD, SEQ]), at("merged_T_lo", 160, [128, KD, SEQ], F32R)
        mT_hi = at("merged_T_hi", 120, [128, KD, SEQ], F32R)
        mtmp = at("mtmp", 184, [128, 2, 512])
        WO_RAW, WO_HI = (16, 24, 188, 32), (80, 88, 112, 40)
        wo = [at(f"w_out_{j}", WO_RAW[j], [128, SLOT]) for j in range(4)]
        wo_lo = [at(f"w_out_lo_{j}", WO_RAW[j], [128, SLOT], F32R) for j in range(4)]
        wo_hi = [at(f"w_out_hi_{j}", WO_HI[j], [128, SLOT], F32R) for j in range(4)]
        xn2_a, xn2_b = at("xn2_a", 136, [128, 2, D]), at("xn2_b", 176, [128, 2, D])
        xn2 = [(xn2_a, xn2_b)[c // 2][:, c % 2, :] for c in range(NT)]
        h2T = at("h2T", 104, [128, 2, KD, 128])
        bias32 = at("bias32", 36, [128, 3 * D])
        bias_new = at("bias_new", 48, [128, 3 * D], BF16)
        bias_tab = at("bias_tab", 190, [128, 3 * D], BF16)
        xg_t = at("xg", 160, [CAP, D])
        hid_t = at("hid", 164, [CAP, FF])
        ysb_t = at("y", 168, [CAP, D])
        gc_t = at("gate_half", 172, [CAP, 512])
        uc_t = at("up_half", 174, [CAP, 512])
        sg_t = at("sig_half", 176, [CAP, 512])
        XT = at("XT", 178, [128, 2, KD, CAP], F32R)
        hidT = at("hidT", 184, [128, 2, KD, CAP], F32R)
        fin = at("fin", 0, [128, NT, D])
        fin_sq = at("fin_sq", 16, [128, NT, D])
        gfin_t = at("g_final_rows", 32, [128, D])
        rt1, rt2, gfin = rt1_t[:, :], rt2_t[:, :], gfin_t[:, :]
        xg, hid, ysb, gc, uc, sg = xg_t[:, :], hid_t[:, :], ysb_t[:, :], gc_t[:, :], uc_t[:, :], sg_t[:, :]

        ident = sb("ident", [128, 128])
        identb = sb("identb", [128, 128], BF16)
        mask_lo = sb("mask_lo", [128, 128], BF16)
        mask_hi = sb("mask_hi", [128, 128], BF16)
        mask_all = sb("mask_all", [128, 128], BF16)
        tri = sb("tri", [128, 128], BF16)
        onesb = sb("onesb", [128, 128], BF16)
        iota_cap = sb("iota_cap", [128, CAP])
        part_mod = sb("part_mod", [128, CAP])
        erow = sb("erow", [128, E])
        passoff = sb("passoff", [128, 8])
        idle_row = sb("idle_row", [128, 1])
        idle_neg = sb("idle_neg", [128, 1])
        feats = sb("feats", [128, NT, E, 6], BF16)
        shared = sb("shared", [128, 512])
        rp = shared[:, :].rearrange("p (c t n) -> p c t n", t=4, n=32)
        posx = shared[:, 0:128].rearrange("p (c e) -> p c e", e=E)
        ex = shared[:, 128:256].rearrange("p (c e) -> p c e", e=E)
        onehot = shared[:, 256:256 + 2 * CAP].bitcast(BF16).rearrange("p (c n) -> p c n", n=CAP)
        gains = sb("gains", [128, 2, HD])
        sink = sb("sink", [128, 8])
        brt = sb("brt", [128, E])
        gcol = sb("gcol", [128, KD])
        eps = sb("eps", [128, 1])
        warm = sb("warm", [128, 1])
        ss = sb("ss", [128, NT])
        rstd = sb("rstd", [128, NT])
        hs = sb("hs", [128, NT, 12])
        mx = sb("mx", [128, 4])
        negm = sb("negm", [128, 2, 4])
        esink = sb("esink", [128, 2, 4])
        psum_p = sb("psum_p", [128, 2, 4])
        rinv = sb("rinv", [128, 4])
        lg = sb("lg", [128, NT, E])
        m8 = sb("m8", [128, 8])
        m8x = sb("m8x", [128, 8])
        repl = sb("repl", [128, E])
        mask = sb("mask", [128, NT, E], BF16)
        negl = sb("negl", [128, NT])
        gsum = sb("gsum", [128, NT])
        cmax = sb("cmax", [128, 1])
        over = sb("over", [128, 8])
        npass = sb("npass", [128, 1])
        items_i = sb("items_i", [128, 2], I32)
        tgt = sb("tgt", [128, NT])
        sel = sb("sel", [96, CAP], BF16)
        f6 = sb("f6", [CAP, 6])
        s1 = sb("s1", [CAP, 1])
        s2 = sb("s2", [CAP, 1])
        idx = sb("idx", [CAP, 4], I32)
        gates = sb("gates", [CAP, 4])
        gate_c = sb("gate_c", [CAP, 1])

        assert nc.sbuf_base <= ARENA
        ps = ctx.enter_context(nc.psum_tensor("ps", [128, 8, 512], F32))
        idx_ps = ps[0:CAP, 7, 448:454]

        ADDED = 3 * 16
        x_in = [sem(f"x_in{c}") for c in range(NT)]
        g_mix_in = sem("g_mix_in")
        consts_in = sem("consts_in")
        late_in = sem("late_in")
        chunk_in = [sem(f"chunk_in{s}") for s in range(NIN)]
        wo_in = [sem(f"wo_in{s}") for s in range(4)]
        expert_in = [sem(f"expert_in{s}") for s in range(NCH)]
        in_hi = sem("in_hi")
        in_lo = sem("in_lo")
        in_used = sem("in_used")
        branches_used = sem("branches_used")
        ex_hi = sem("ex_hi")
        ex_lo = sem("ex_lo")
        ex_used = sem("ex_used")
        pool_step = sem("pool_step")
        eps_set = sem("eps_set")
        ident_set = sem("ident_set")
        pool_past = sem("pool_past")
        zero_set = sem("zero_set")
        pool_consts = sem("pool_consts")
        part_mod_set = sem("part_mod_set")
        gcol_ps = sem("gcol_ps")
        gcol_ready = sem("gcol_ready")
        sq_done = sem("sq_done")
        rt_done = sem("rt_done")
        dve_step = sem("dve_step")
        xn_ready = sem("xn_ready")
        hT_ps = sem("hT_ps")
        hT_hi = sem("hT_hi")
        hT_lo = sem("hT_lo")
        proj_ps = sem("proj_ps")
        proj_out = sem("proj_out")
        hs_ready = sem("hs_ready")
        hrt_done = sem("hrt_done")
        rope_done = sem("rope_done")
        qT_ps = sem("qT_ps")
        qT_a = sem("qT_a")
        qT_d = sem("qT_d")
        scores_ps = sem("scores_ps")
        negm_ready = sem("negm_ready")
        exps_done = sem("exps_done")
        esink_done = sem("esink_done")
        diag_ready = sem("diag_ready")
        pT_ps = sem("pT_ps")
        pT_a = sem("pT_a")
        pT_d = sem("pT_d")
        pv_ps = sem("pv_ps")
        oT_out = sem("oT_out")
        branch_ps = sem("branch_ps")
        merged = sem("merged")
        br_hi_done = sem("br_hi_done")
        br_lo_done = sem("br_lo_done")
        oT_hi = sem("oT_hi")
        oT_lo = sem("oT_lo")
        mT_hi_done = sem("mT_hi_done")
        mT_lo_done = sem("mT_lo_done")
        wo_hi_done = sem("wo_hi_done")
        wo_lo_done = sem("wo_lo_done")
        wout_ps = sem("wout_ps")
        x1_ready = sem("x1_ready")
        sq2_done = sem("sq2_done")
        rt2_done = sem("rt2_done")
        xn2_ready = sem("xn2_ready")
        rows_stored = sem("rows_stored")
        h2T_ps = sem("h2T_ps")
        h2T_a = sem("h2T_a")
        h2T_d = sem("h2T_d")
        logits_ps = sem("logits_ps")
        lg_ready = sem("lg_ready")
        ex_done = sem("ex_done")
        mask_ready = sem("mask_ready")
        pos_ps = sem("pos_ps")
        route_ready = sem("route_ready")
        items_ready = sem("items_ready")
        bias_in = sem("bias_in")
        bias_ready = sem("bias_ready")
        bias_back = sem("bias_back")
        onehot_ready = sem("onehot_ready")
        idx_done = sem("idx_done")
        idx_ready = sem("idx_ready")
        gathered = sem("gathered")
        scattered = sem("scattered")
        xt_ps = sem("xt_ps")
        xt_hi = sem("xt_hi")
        xt_lo = sem("xt_lo")
        sel_ready = sem("sel_ready")
        gate_ready = sem("gate_ready")
        pair_ps = sem("pair_ps")
        clamp_ready = sem("clamp_ready")
        sig_done = sem("sig_done")
        hid_ready = sem("hid_ready")
        hidT_ps = sem("hidT_ps")
        hidT_hi = sem("hidT_hi")
        hidT_lo = sem("hidT_lo")
        down_begun = sem("down_begun")
        y_ready = sem("y_ready")
        acc_in = [sem(f"acc_in{c}") for c in range(NT)]
        gfin_in = sem("gfin_in")
        fsq_done = sem("fsq_done")
        frt_done = sem("frt_done")
        out_ready = sem("out_ready")
        out_stored = sem("out_stored")

        def kp(ap):
            return ap.rearrange("(k p) n -> p k n", p=128)

        IN_CHUNKS, CHUNKS = 14, 18
        chunk_src = [kp(w_in[0, s * 512:(s + 1) * 512, g * 512:(g + 1) * 512]) for g in range(7) for s in range(2)]
        chunk_src += [kp(w[0, :, h * 512:(h + 1) * 512]) for h in range(2) for w in (w_branch_a, w_branch_b)]

        def blocks(t, width):
            return t.rearrange("p (k n) -> p k n", n=width)

        def expert_src(e, s):
            if s < 8:
                half, k2 = s // 4, s % 4
                w = w_gate_up[0, e, k2 * 256:(k2 + 1) * 256, :].rearrange("(p k) (t n) -> p (k t) n", k=2, t=2)
                return w[:, :, half * 512:(half + 1) * 512]
            return w_down[0, e, (s - 8) * 256:(s - 7) * 256, :].rearrange("(p k) n -> p (k n)", k=2)

        def raw_slot(i, s):
            n = (i * NCH + s + NRAW - 2) % NRAW
            return raw[:, n, :] if isinstance(n, int) else raw[:, bass.ds(n, 1), :].rearrange("p one n -> p (one n)")

        def load_expert(sp, i, s, e):
            dst = raw_slot(i, s)
            if s < 8:
                dst = dst.rearrange("p (a n) -> p a n", a=4)
            sp.dma_start(dst, expert_src(e, s)).then_inc(expert_in[s], 16)

        def expert_w(s, part, k, t):
            return split[:, s % NSPLIT, part, (2 * k + t) * 512:(2 * k + t + 1) * 512]

        def window(n):
            return [kb for kb in (n - 1, n, n + 1) if 0 <= kb < NT]

        WW = 384

        block = ctx.enter_context(nc.Block())

        @block.sync
        def _(sp):
            x_v = x.rearrange("b (c p) n -> (b c) p n", p=128)
            for c in range(NT):
                sp.dma_start(xs[:, c, :], x_v[c]).then_inc(x_in[c], 16)
            for n in range(CHUNKS):
                if n >= NIN:
                    sp.wait_ge(in_lo, n - NIN + 1)
                w = chunk_src[n]
                sp.dma_start(blocks(raw[:, n % NIN, :], w.shape[2]), w).then_inc(chunk_in[n % NIN], 16)
            def load_wo(j):
                sp.dma_start(blocks(wo[j][:, :], D), kp(w_out[0, j * 256:(j + 1) * 256, :])).then_inc(wo_in[j], 16)

            sp.wait_ge(pv_ps, JOBS)
            load_wo(2)
            sp.wait_ge(branch_ps, KD // 2)
            load_wo(0)
            load_wo(1)
            sp.wait_ge(merged, KD // 2)
            load_wo(3)
            load_expert(sp, 0, 0, 0)
            sp.wait_ge(merged, KD)
            load_expert(sp, 0, 1, 0)
            sp.wait_ge(branches_used, 1)
            load_expert(sp, 0, 2, 0)
            load_expert(sp, 0, 3, 0)
            sp.wait_ge(wout_ps, 2 * NT)
            sp.wait_ge(scattered, ADDED)
            sp.dma_start(bias_tab[0:96, :], bias_parts).then_inc(bias_back, 16)
            for s in range(4, NRAW):
                load_expert(sp, 0, s, 0)
            for s in range(NRAW, NCH):
                sp.wait_ge(ex_lo, s - NRAW + 1)
                load_expert(sp, 0, s, 0)
            sp.wait_ge(items_ready, 1)
            items = sp.value_load(items_i[0:1, 0:1], min_val=E, max_val=E * PASSES)
            with sp.Fori(1, items) as i:
                for s in range(NCH):
                    sp.wait_ge(ex_lo, i * NCH + s - NRAW + 1)
                    load_expert(sp, i, s, i % E)
            sp.wait_ge(scattered, items * 16 + ADDED)
            acc_v = acc[0:SEQ, :].rearrange("(c p) n -> c p n", p=128)
            out_v = out.rearrange("b (c p) n -> (b c) p n", p=128)
            for c in range(NT):
                sp.dma_start(fin[:, c, :], acc_v[c]).then_inc(acc_in[c], 16)
            for c in range(NT):
                sp.wait_ge(out_ready, c + 1)
                sp.dma_start(out_v[c], fin[:, c, :]).then_inc(out_stored, 16)
            sp.wait_ge(out_stored, 16 * NT)

        @block.gpsimd
        def _(pool):
            g = nc.gpsimd
            g.memset(eps[:, :], EPS).then_inc(eps_set, 1)
            g.memset(ident[:, :], 0.0).then_inc(pool_step, 1)
            pool.wait_ge(pool_step, 1)
            g.affine_select(out=ident[:, :], in_=ident[:, :], compare_op=ALU.not_equal, fill=1.0, base=0,
                            pattern=[[-1, 128]], channel_multiplier=1).then_inc(ident_set, 1)
            g.memset(zeros[:, :], 0.0).then_inc(zero_set, 1)
            g.memset(identb[:, :], 0.0)
            g.memset(mask_lo[:, :], 0.0)
            g.memset(mask_hi[:, :], 0.0)
            g.memset(mask_all[:, :], NEG)
            g.memset(tri[:, :], 1.0)
            g.memset(onesb[:, :], 1.0)
            g.memset(part_mod[:, :], 999.0)
            g.memset(feats[:, :, :, 2:3], 1.0).then_inc(pool_step, 1)
            pool.wait_ge(pool_step, 2)
            g.affine_select(out=identb[:, :], in_=identb[:, :], compare_op=ALU.not_equal, fill=1.0, base=0,
                            pattern=[[-1, 128]], channel_multiplier=1)
            g.affine_select(out=mask_lo[:, :], in_=mask_lo[:, :], compare_op=ALU.is_ge, fill=NEG, base=0,
                            pattern=[[1, 128]], channel_multiplier=-1)
            g.affine_select(out=mask_hi[:, :], in_=mask_hi[:, :], compare_op=ALU.is_ge, fill=NEG, base=0,
                            pattern=[[-1, 128]], channel_multiplier=1)
            g.affine_select(out=tri[:, :], in_=tri[:, :], compare_op=ALU.is_ge, fill=0.0, base=-1,
                            pattern=[[1, 128]], channel_multiplier=-1)
            g.iota(iota_cap[:, :], pattern=[[1, CAP]], base=0, channel_multiplier=0,
                   allow_small_or_imprecise_dtypes=True)
            g.iota(erow[:, :], pattern=[[1, E]], base=0, channel_multiplier=0, allow_small_or_imprecise_dtypes=True)
            g.iota(passoff[:, :], pattern=[[CAP, 8]], base=0, channel_multiplier=0,
                   allow_small_or_imprecise_dtypes=True)
            g.iota(idle_row[:, :], pattern=[[0, 1]], base=SEQ, channel_multiplier=1,
                   allow_small_or_imprecise_dtypes=True)
            g.iota(idle_neg[:, :], pattern=[[0, 1]], base=-SEQ, channel_multiplier=-1,
                   allow_small_or_imprecise_dtypes=True)
            g.iota(feats[:, :, :, 0:1], pattern=[[0, NT], [0, E], [0, 1]], base=0, channel_multiplier=1,
                   allow_small_or_imprecise_dtypes=True)
            g.iota(feats[:, :, :, 1:2], pattern=[[128, NT], [0, E], [0, 1]], base=0, channel_multiplier=0,
                   allow_small_or_imprecise_dtypes=True).then_inc(pool_consts, 1)
            pool.wait_ge(pool_consts, 1)
            for q in range(3):
                g.iota(part_mod[32 * q:32 * q + 32, :], pattern=[[0, CAP]], base=0, channel_multiplier=1,
                       allow_small_or_imprecise_dtypes=True).then_inc(part_mod_set, 1)
                pool.wait_ge(part_mod_set, q + 1)
            pool.wait_ge(zero_set, 1)
            pool.dma_start(h2buf[SEQ:ROWS, :], zeros[:, :]).then_inc(scattered, 16)
            pool.dma_start(acc[SEQ:ROWS, :], zeros[:, :]).then_inc(scattered, 16)

            for q in range(3):
                rows = slice(32 * q, 32 * q + 32)
                pool.dma_start(bias32[rows, 0:2 * FF], b_gate_up[0]).then_inc(bias_in, 16)
                pool.dma_start(bias32[rows, 2 * FF:3 * FF], b_down[0]).then_inc(bias_in, 16)
            pool.wait_ge(bias_in, 96)
            chain = [2]

            def link(ins):
                chain[0] += 1
                ins.then_inc(pool_step, 1)
                pool.wait_ge(pool_step, chain[0])

            part1, part2 = slice(32, 64), slice(64, 96)
            link(g.tensor_copy(bias_new[0:96, :], bias32[0:96, :]))
            for rows in (part1, part2):
                link(g.tensor_tensor(bias32[rows, :], bias32[rows, :], bias_new[rows, :], ALU.subtract))
                link(g.tensor_copy(bias_new[rows, :], bias32[rows, :]))
            link(g.tensor_tensor(bias32[part2, :], bias32[part2, :], bias_new[part2, :], ALU.subtract))
            g.tensor_copy(bias_new[part2, :], bias32[part2, :]).then_inc(bias_ready, 1)
            pool.wait_ge(bias_ready, 1)
            pool.dma_start(bias_parts, bias_new[0:96, :]).then_inc(scattered, 16)

            pool.wait_ge(rows_stored, 2 * NT * 16)
            pool.wait_ge(scattered, ADDED)

            def gather(col):
                g.indirect_dma_start(out=xg, out_offset=None, in_=h2buf,
                                     in_offset=bass.IndirectOffsetOnAxis(ap=idx[:, col:col + 1], axis=0)
                                     ).then_inc(gathered, 16)

            pool.wait_ge(idx_ready, 1)
            gather(0)
            pool.wait_ge(items_ready, 1)
            items = pool.value_load(items_i[0:1, 0:1], min_val=E, max_val=E * PASSES)
            with pool.Fori(0, items, 4) as i4:
                for u in range(4):
                    pool.wait_ge(idx_ready, i4 + u + 2)
                    pool.wait_ge(xt_ps, i4 + u + 1)
                    pool.sem_inc(pool_past, 1)
                    gather((u + 1) % 4)
                    pool.wait_ge(scattered, 16 * (i4 + u) + ADDED)
                    pool.wait_ge(y_ready, 2 * (i4 + u) + 3)
                    pool.sem_inc(pool_past, 1)
                    g.indirect_dma_start(out=acc, out_offset=bass.IndirectOffsetOnAxis(ap=idx[:, u:u + 1], axis=0),
                                         in_=ysb, in_offset=None, compute_op=ALU.add).then_inc(scattered, 16)

        @block.scalar
        def _(act):
            a = nc.scalar
            act.dma_start(g16[0:8, :], g_mix.rearrange("l (k p) -> (l k) p", p=128)).then_inc(g_mix_in, 16)
            act.wait_ge(eps_set, 1)
            a.activation(warm[:, :], eps[:, :], ACT.Sqrt)
            for c in range(NT):
                act.wait_ge(x_in[c], 16)
                a.activation(xn[:, c, :], xs[:, c, :], ACT.Square, accum_out=ss[:, c:c + 1]).then_inc(sq_done, 1)
                act.wait_ge(sq_done, c + 1)
                a.activation(ss[:, c:c + 1], ss[:, c:c + 1], ACT.Sqrt, bias=eps[:, 0:1],
                             scale=1.0 / D).then_inc(rt_done, 1)
            act.dma_start(rp, rope.rearrange("(c p) t n -> p c t n", p=128)).then_inc(consts_in, 16)
            act.dma_start(gains[:, 0, :], qa_norm[0:1, :].to_broadcast([128, HD])).then_inc(consts_in, 16)
            act.dma_start(gains[:, 1, :], ka_norm[0:1, :].to_broadcast([128, HD])).then_inc(consts_in, 16)
            act.dma_start(sink[:, :], sink_b[0:1, :].to_broadcast([128, 8])).then_inc(consts_in, 16)
            act.dma_start(brt[:, :], b_router[0:1, :].to_broadcast([128, E])).then_inc(consts_in, 16)

            def in_split_hi(n):
                if n >= IN_CHUNKS:
                    return
                act.wait_ge(chunk_in[n % NIN], 16 * (n // NIN + 1))
                if n >= NIN_SPLIT:
                    act.wait_ge(in_used, n - NIN_SPLIT + 1)
                a.activation(split[:, n % NIN_SPLIT, 0, :], raw[:, n % NIN, :], ACT.Copy).then_inc(in_hi, 1)

            in_split_hi(0)
            act.wait_ge(gcol_ready, 1)
            for k in range(KD):
                act.wait_ge(hT_ps, k + 1)
                a.activation(hT[:, 0, k, :], ps[:, k, :], ACT.Copy, scale=gcol[:, k:k + 1]).then_inc(hT_hi, 1)
                if k % 4 == 3:
                    in_split_hi(1 + k // 4)

            def project_out(n):
                grp, c = n // NT, n % NT
                act.wait_ge(proj_ps, n + 1)
                src = ps[:, n % 4, :]
                if grp >= 3:
                    a.activation(gT[:, n - 12, :], src, ACT.Sigmoid).then_inc(proj_out, 1)
                    return
                if grp == 0:
                    a.activation(qk[:, c, 0:512], src, ACT.Copy).then_inc(proj_out, 1)
                    return
                if grp == 1:
                    kv, q, q_at, k_at, v_at = src[:, 0:256], src[:, 256:512], 768, 512, 0
                else:
                    kv, q, q_at, k_at, v_at = src[:, 256:512], src[:, 0:256], 1024, 1280, 128
                a.activation(qk[:, c, q_at:q_at + 256], q, ACT.Copy)
                k_dst = qk[:, c, k_at:k_at + 256].rearrange("p (h two n) -> p h two n", h=2, two=2)
                k_src = kv[:, 0:128].rearrange("p (h n) -> p h n", h=2)
                a.activation(k_dst[:, :, 0, :], k_src, ACT.Copy)
                a.activation(k_dst[:, :, 1, :], k_src, ACT.Copy)
                a.activation(v_sb[:, c, v_at:v_at + 128], kv[:, 128:256], ACT.Copy).then_inc(proj_out, 1)

            act.wait_ge(xn_ready, NT)
            act.wait_ge(hT_ps, KD)
            for grp in range(7):
                if grp == 3:
                    act.wait_ge(scattered, ADDED)
                if grp:
                    in_split_hi(2 * grp + 2)
                project_out(4 * grp)
                if grp >= 3:
                    c = grp - 3
                    act.wait_ge(hs_ready, c + 1)
                    a.activation(hs[:, c, :], hs[:, c, :], ACT.Sqrt, bias=eps[:, 0:1],
                                 scale=1.0 / HD).then_inc(hrt_done, 1)
                project_out(4 * grp + 1)
                project_out(4 * grp + 2)
                in_split_hi(2 * grp + 3)
                project_out(4 * grp + 3)
            act.wait_ge(in_used, IN_CHUNKS)
            act.dma_start(wr[:, :, :], kp(w_router[0])).then_inc(late_in, 16)
            act.dma_start(gffn[:, :], g_ffn[0:1, :].to_broadcast([128, D])).then_inc(late_in, 16)
            for n in range(1, 12, 2):
                act.wait_ge(qT_ps, n + 1)
                c, t = n // 3, n % 3
                a.activation(qT[:, 4 * t:4 * t + 4, c * 128:(c + 1) * 128],
                             ps[:, 4 + t, :].rearrange("p (t n) -> p t n", n=128), ACT.Copy).then_inc(qT_a, 1)

            def exps(j):
                w = SEQ if j < 8 else WW
                act.wait_ge(negm_ready, j + 1)
                if j >= 2:
                    act.wait_ge(pT_ps, 4 * (j - 1))
                for n in range(4):
                    a.activation(probs[:, j % 2, n, 0:w], ps[:, n, 0:w], ACT.Exp, bias=negm[:, j % 2, n:n + 1],
                                 scale=SCALE, accum_out=psum_p[:, j % 2, n:n + 1]).then_inc(exps_done, 1)
                if j >= 8:
                    a.activation(esink[:, j % 2, :], negm[:, j % 2, :], ACT.Exp,
                                 bias=sink[:, j - 8:j - 7]).then_inc(esink_done, 1)

            def branch_hi(n):
                m = n % NIN
                act.wait_ge(chunk_in[m], 16 * (n // NIN + 1))
                a.activation(br_hi[:, m, :], raw[:, m, :], ACT.Copy).then_inc(br_hi_done, 1)

            def oT_b_hi(p):
                act.wait_ge(oT_out, 5 + p)
                a.activation(oTb_hi[:, p, :], oTb[:, p, :], ACT.Copy).then_inc(oT_hi, 1)

            exps(0)
            for j in range(JOBS):
                for kb in range(2):
                    act.wait_ge(pT_ps, 4 * j + kb + 1)
                    if j:
                        act.wait_ge(pv_ps, j)
                    q0, q1 = (0, NT) if j < 8 else (window(kb)[0], window(kb)[-1] + 1)
                    a.activation(pT[:, kb, q0 * 128:q1 * 128], ps[:, 4 + (4 * j + kb) % 3, q0 * 128:q1 * 128],
                                 ACT.Copy).then_inc(pT_a, 1)
                if j + 1 < JOBS:
                    exps(j + 1)
                if j < 4:
                    branch_hi(IN_CHUNKS + j)
                if j == 8:
                    act.wait_ge(oT_out, 4)
                    a.activation(oTa_hi[:, :, :], oTa[:, :, :], ACT.Copy).then_inc(oT_hi, 1)
                if j >= 10 and j % 2 == 0:
                    oT_b_hi((j - 10) // 2)
            oT_b_hi(3)
            def wo_split_hi(j):
                act.wait_ge(wo_in[j], 16)
                a.activation(wo_hi[j][:, :], wo[j][:, :], ACT.Copy).then_inc(wo_hi_done, 1)

            for c in range(KD):
                act.wait_ge(merged, c + 1)
                a.activation(mT_hi[:, c, :], mT[:, c, :], ACT.Copy).then_inc(mT_hi_done, 1)
                if c in (4, 5):
                    wo_split_hi(c - 4)
            act.wait_ge(branch_ps, KD)
            wo_split_hi(2)
            wo_split_hi(3)

            def h2T_half(c):
                act.wait_ge(h2T_ps, c + 1)
                if c >= 2:
                    act.wait_ge(logits_ps, c - 1)
                a.activation(h2T[:, c % 2, 0:4, :], ps[:, 0, :].rearrange("p (k n) -> p k n", n=128),
                             ACT.Copy).then_inc(h2T_a, 1)

            def ex_split_hi(i, s):
                act.wait_ge(expert_in[s], (i + 1) * 16)
                act.wait_ge(ex_used, i * NCH + s + 1)
                a.activation(split[:, s % NSPLIT, 0, :], raw_slot(i, s), ACT.Copy).then_inc(ex_hi, 1)

            act_v = acc[0:SEQ, :].rearrange("(c p) n -> c p n", p=128)
            h2_v = h2buf[0:SEQ, :].rearrange("(c p) n -> c p n", p=128)
            def root(c):
                act.wait_ge(x1_ready, 2 * c + 2)
                act.dma_start(act_v[c], xs[:, c, :]).then_inc(rows_stored, 16)
                a.activation(xn2[c], xs[:, c, :], ACT.Square, accum_out=ss[:, c:c + 1]).then_inc(sq2_done, 1)
                act.wait_ge(sq2_done, c + 1)
                a.activation(ss[:, c:c + 1], ss[:, c:c + 1], ACT.Sqrt, bias=eps[:, 0:1],
                             scale=1.0 / D).then_inc(rt2_done, 1)

            def store_rows(c):
                act.wait_ge(xn2_ready, c + 1)
                act.dma_start(h2_v[c], xn2[c]).then_inc(rows_stored, 16)

            def top_exp(c):
                act.wait_ge(lg_ready, c + 1)
                a.activation(ex[:, c, :], lg[:, c, :], ACT.Exp, bias=negl[:, c:c + 1]).then_inc(ex_done, 1)

            root(0)
            root(1)
            store_rows(0)
            store_rows(1)
            root(2)
            h2T_half(0)
            store_rows(2)
            h2T_half(1)
            ex_split_hi(0, 0)
            root(3)
            h2T_half(2)
            a.activation(warm[:, :], eps[:, :], ACT.Exp)
            store_rows(3)
            top_exp(0)
            top_exp(1)
            top_exp(2)
            h2T_half(3)
            ex_split_hi(0, 1)
            top_exp(3)
            act.wait_ge(logits_ps, NT)
            ex_split_hi(0, 2)
            ex_split_hi(0, 3)
            act.wait_ge(rows_stored, 2 * NT * 16)
            ex_split_hi(0, 4)
            ex_split_hi(0, 5)

            def rows_hi(n):
                act.wait_ge(xt_ps, n)
                for t in range(2):
                    last = a.activation(XT[:, 0, 4 * t:4 * t + 4, :],
                                        ps[:, t, 0:4 * CAP].rearrange("p (k n) -> p k n", n=CAP), ACT.Copy)
                last.then_inc(xt_hi, 1)

            def hidden_hi(half, n):
                act.wait_ge(hidT_ps, n)
                a.activation(hidT[:, 0, 4 * half:4 * half + 4, :],
                             ps[:, 6 + half, 0:4 * CAP].rearrange("p (k n) -> p k n", n=CAP),
                             ACT.Copy).then_inc(hidT_hi, 1)

            rows_hi(1)
            act.wait_ge(items_ready, 1)
            last_item = act.value_load(items_i[0:1, 1:2], min_val=E - 1, max_val=E * PASSES - 1)
            act.sem_inc(y_ready, 1)

            def act_item(i, nxt):
                a.activation(warm[:, :], eps[:, :], ACT.Sigmoid)
                for s in (6, 7, 8):
                    ex_split_hi(i, s)
                act.wait_ge(clamp_ready, 2 * i + 1)
                a.activation(sg, gc, ACT.Sigmoid, scale=1.702).then_inc(sig_done, 1)
                for s in (9, 10, 11):
                    ex_split_hi(i, s)
                hidden_hi(0, 2 * i + 2)
                if nxt:
                    ex_split_hi(i + 1, 0)
                act.wait_ge(clamp_ready, 2 * i + 2)
                a.activation(sg, gc, ACT.Sigmoid, scale=1.702).then_inc(sig_done, 1)
                if nxt:
                    ex_split_hi(i + 1, 1)
                hidden_hi(1, 2 * i + 3)
                act.wait_ge(pair_ps, 2 * i + 2)
                rows_hi(i + 2)
                if nxt:
                    for s in (2, 3, 4, 5):
                        ex_split_hi(i + 1, s)
                act.wait_ge(ex_used, (i + 1) * NCH + NSPLIT)
                act.wait_ge(gate_ready, i + 1)
                act.wait_ge(scattered, 16 * i + ADDED)
                for t in range(2):
                    a.activation(ysb[:, t * 512:(t + 1) * 512], ps[0:CAP, 4 + t, :], ACT.Copy,
                                 scale=gate_c[:, 0:1]).then_inc(y_ready, 1)

            with act.Fori(0, last_item) as i:
                act_item(i, True)
            act_item(last_item, False)

            a.activation(warm[:, :], eps[:, :], ACT.Sqrt)
            act.dma_start(gfin, g_final.rearrange("(l n) -> l n", l=1).to_broadcast([128, D])).then_inc(gfin_in, 16)
            for c in range(NT):
                act.wait_ge(acc_in[c], 16)
                a.activation(fin_sq[:, c, :], fin[:, c, :], ACT.Square, accum_out=ss[:, c:c + 1]).then_inc(fsq_done, 1)
                act.wait_ge(fsq_done, c + 1)
                a.activation(ss[:, c:c + 1], ss[:, c:c + 1], ACT.Sqrt, bias=eps[:, 0:1],
                             scale=1.0 / D).then_inc(frt_done, 1)

        @block.vector
        def _(dve):
            v = nc.vector
            steps = [0]

            def link(ins):
                steps[0] += 1
                ins.then_inc(dve_step, 1)
                dve.wait_ge(dve_step, steps[0])

            for c in range(NT):
                dve.wait_ge(rt_done, c + 1)
                link(v.reciprocal(rstd[:, c:c + 1], ss[:, c:c + 1]))
                v.tensor_scalar(xn[:, c, :], xs[:, c, :], rstd[:, c:c + 1], None, ALU.mult).then_inc(xn_ready, 1)
                if c == 0:
                    dve.wait_ge(gcol_ps, 1)
                    v.tensor_copy(gcol[:, :], ps[:, 7, 0:KD]).then_inc(gcol_ready, 1)
            dve.wait_ge(gcol_ready, 1)

            def in_split_lo(n):
                if n >= IN_CHUNKS:
                    return
                dve.wait_ge(in_hi, n + 1)
                v.tensor_tensor(split[:, n % NIN_SPLIT, 1, :], raw[:, n % NIN, :],
                                split[:, n % NIN_SPLIT, 0, :].bitcast(F32), ALU.subtract).then_inc(in_lo, 1)

            in_split_lo(0)
            for k in range(KD):
                dve.wait_ge(hT_hi, k + 1)
                v.scalar_tensor_tensor(out=hT[:, 1, k, :], in0=ps[:, k, :], scalar=gcol[:, k:k + 1],
                                       in1=hT[:, 0, k, :].bitcast(F32), op0=ALU.mult,
                                       op1=ALU.subtract).then_inc(hT_lo, 1)
                if k % 4 == 3:
                    in_split_lo(1 + k // 4)
            for n in range(NIN_SPLIT, 8):
                in_split_lo(n)
            dve.wait_ge(consts_in, 80)
            for c in range(NT):
                dve.wait_ge(proj_out, 8 + c + 1)
                in_split_lo(2 * c + 8)
                if c:
                    dve.wait_ge(rope_done, c)
                qa = qk[:, c, 0:768].rearrange("p (h n) -> p h n", n=HD)
                link(v.tensor_tensor(rt1, qk[:, c, 0:768], qk[:, c, 0:768], ALU.mult))
                v.tensor_reduce(hs[:, c, :], rt1.rearrange("p (h n) -> p h n", n=HD), AX.X,
                                ALU.add).then_inc(hs_ready, 1)
                dve.wait_ge(hrt_done, c + 1)
                link(v.reciprocal(hs[:, c, :], hs[:, c, :]))
                link(v.tensor_tensor(qa, qa, hs[:, c, :].unsqueeze(2).to_broadcast([128, 12, HD]), ALU.mult))
                v.tensor_tensor(qa[:, 0:8, :], qa[:, 0:8, :],
                                gains[:, 0:1, :].to_broadcast([128, 8, HD]), ALU.mult)
                link(v.tensor_tensor(qa[:, 8:12, :], qa[:, 8:12, :],
                                     gains[:, 1:2, :].to_broadcast([128, 4, HD]), ALU.mult))
                last = None
                for br in range(2):
                    h = qk[:, c, br * 768:(br + 1) * 768].rearrange("p (h two n) -> p h two n", two=2, n=32)
                    x1, x2 = h[:, :, 0, :], h[:, :, 1, :]
                    cos = rp[:, c, 2 * br:2 * br + 1, :].to_broadcast([128, 12, 32])
                    sin = rp[:, c, 2 * br + 1:2 * br + 2, :].to_broadcast([128, 12, 32])
                    t1 = rt1[:, br * 384:(br + 1) * 384].rearrange("p (h n) -> p h n", n=32)
                    t2 = rt2[:, br * 384:(br + 1) * 384].rearrange("p (h n) -> p h n", n=32)
                    v.tensor_tensor(t1, x1, sin, ALU.mult)
                    link(v.tensor_tensor(t2, x2, sin, ALU.mult))
                    v.tensor_tensor(x1, x1, cos, ALU.mult)
                    link(v.tensor_tensor(x2, x2, cos, ALU.mult))
                    v.tensor_tensor(x1, x1, t2, ALU.subtract)
                    last = v.tensor_tensor(x2, x2, t1, ALU.add)
                last.then_inc(rope_done, 1)
                in_split_lo(2 * c + 9)
            for n in range(0, 12, 2):
                dve.wait_ge(qT_ps, n + 1)
                c, t = n // 3, n % 3
                v.tensor_copy(qT[:, 4 * t:4 * t + 4, c * 128:(c + 1) * 128],
                              ps[:, 4 + t, :].rearrange("p (t n) -> p t n", n=128)).then_inc(qT_d, 1)

            def row_max(j):
                w = SEQ if j < 8 else WW
                dve.wait_ge(scores_ps, j + 1)
                if j:
                    dve.wait_ge(negm_ready, j)
                link(v.reduce_max(mx[:, :], ps[:, 0:4, 0:w], AX.X))
                if j < 8:
                    v.tensor_scalar(negm[:, j % 2, :], mx[:, :], -SCALE, None, ALU.mult).then_inc(negm_ready, 1)
                else:
                    link(v.tensor_scalar(mx[:, :], mx[:, :], SCALE, sink[:, j - 8:j - 7], ALU.mult, ALU.max))
                    v.tensor_scalar(negm[:, j % 2, :], mx[:, :], -1.0, None, ALU.mult).then_inc(negm_ready, 1)

            def diagonals(j):
                dve.wait_ge(exps_done, 4 * j + 4)
                total = psum_p[:, j % 2, :]
                if j >= 8:
                    dve.wait_ge(esink_done, j - 7)
                    link(v.tensor_tensor(total, total, esink[:, j % 2, :], ALU.add))
                if j:
                    dve.wait_ge(diag_ready, j)
                link(v.reciprocal(rinv[:, :], total))
                if j:
                    dve.wait_ge(pT_ps, 4 * j)
                for n in range(4):
                    last = v.tensor_scalar(diag[:, n, :], ident[:, :], rinv[:, n:n + 1], None, ALU.mult)
                last.then_inc(diag_ready, 1)

            def branch_lo(n):
                m = n % NIN
                dve.wait_ge(br_hi_done, n - IN_CHUNKS + 1)
                v.tensor_tensor(br_lo[:, m, :], raw[:, m, :], br_hi[:, m, :].bitcast(F32),
                                ALU.subtract).then_inc(br_lo_done, 1)

            def oT_b_lo(p):
                dve.wait_ge(oT_hi, 2 + p)
                v.tensor_tensor(oTb_lo[:, p, :], oTb[:, p, :], oTb_hi[:, p, :].bitcast(F32),
                                ALU.subtract).then_inc(oT_lo, 1)

            row_max(0)
            diagonals(0)
            for j in range(JOBS):
                if j + 1 < JOBS:
                    row_max(j + 1)
                for kb in range(2, 4):
                    dve.wait_ge(pT_ps, 4 * j + kb + 1)
                    if j:
                        dve.wait_ge(pv_ps, j)
                    q0, q1 = (0, NT) if j < 8 else (window(kb)[0], window(kb)[-1] + 1)
                    v.tensor_copy(pT[:, kb, q0 * 128:q1 * 128],
                                  ps[:, 4 + (4 * j + kb) % 3, q0 * 128:q1 * 128]).then_inc(pT_d, 1)
                if j + 1 < JOBS:
                    diagonals(j + 1)
                if j % 2:
                    dve.wait_ge(pv_ps, j + 1)
                    v.tensor_copy((oTa if j < 8 else oTb)[:, j // 2 % 4, :], ps[:, 7, :]).then_inc(oT_out, 1)
                if j < 4:
                    branch_lo(IN_CHUNKS + j)
                if j == 9:
                    dve.wait_ge(oT_hi, 1)
                    v.tensor_tensor(oTa_lo[:, :, :], oTa[:, :, :], oTa_hi[:, :, :].bitcast(F32),
                                    ALU.subtract).then_inc(oT_lo, 1)
                if j >= 11 and j % 2:
                    oT_b_lo((j - 11) // 2)
            oT_b_lo(3)

            def merge_lo(c):
                dve.wait_ge(mT_hi_done, c + 1)
                v.tensor_tensor(mT_lo[:, c, :], mT[:, c, :], mT_hi[:, c, :].bitcast(F32),
                                ALU.subtract).then_inc(mT_lo_done, 1)

            def wo_split_lo(j):
                dve.wait_ge(wo_hi_done, j + 1)
                v.tensor_tensor(wo_lo[j][:, :], wo[j][:, :], wo_hi[j][:, :].bitcast(F32),
                                ALU.subtract).then_inc(wo_lo_done, 1)

            for c in range(KD):
                dve.wait_ge(branch_ps, c + 1)
                b = (c % 2) * 2
                if c >= 2:
                    dve.wait_ge(merged, c - 1)
                v.tensor_tensor(mT[:, c, :], gT[:, c, :], ps[:, b, :], ALU.mult)
                link(v.tensor_tensor(mtmp[:, c % 2, :], gT[:, 8 + c, :], ps[:, b + 1, :], ALU.mult))
                v.tensor_tensor(mT[:, c, :], mT[:, c, :], mtmp[:, c % 2, :], ALU.add).then_inc(merged, 1)
                merge_lo(c)
                if c in (4, 5):
                    wo_split_lo(c - 4)
            wo_split_lo(2)
            wo_split_lo(3)

            def residual(n):
                c, t = n // 2, n % 2
                dve.wait_ge(wout_ps, n + 1)
                half = xs[:, c, t * 512:(t + 1) * 512]
                v.tensor_tensor(half, half, ps[:, 4 + n % 4, :], ALU.add).then_inc(x1_ready, 1)

            def norm(c):
                dve.wait_ge(rt2_done, c + 1)
                if c == 0:
                    dve.wait_ge(late_in, 32)
                link(v.reciprocal(rstd[:, c:c + 1], ss[:, c:c + 1]))
                v.scalar_tensor_tensor(out=xn2[c], in0=xs[:, c, :], scalar=rstd[:, c:c + 1], in1=gffn[:, :],
                                       op0=ALU.mult, op1=ALU.mult).then_inc(xn2_ready, 1)

            def h2_out(c):
                dve.wait_ge(h2T_ps, c + 1)
                if c >= 2:
                    dve.wait_ge(logits_ps, c - 1)
                v.tensor_copy(h2T[:, c % 2, 4:8, :],
                              ps[:, 1, :].rearrange("p (k n) -> p k n", n=128)).then_inc(h2T_d, 1)

            def choose(c):
                dve.wait_ge(logits_ps, c + 1)
                link(v.tensor_tensor(lg[:, c, :], ps[:, 2 + c % 2, c * E:(c + 1) * E], brt[:, :], ALU.add))
                if c:
                    dve.wait_ge(mask_ready, c)
                link(v.max(m8[:, :], lg[:, c, :]))
                v.tensor_scalar(negl[:, c:c + 1], m8[:, 0:1], -1.0, None, ALU.mult).then_inc(lg_ready, 1)
                link(v.tensor_copy(m8x[:, 0:TOPK], m8[:, 0:TOPK]))
                link(v.match_replace(out=repl[:, :], in_to_replace=m8x[:, :], in_values=lg[:, c, :],
                                     imm_value=-3e38))
                v.tensor_scalar(mask[:, c, :], repl[:, :], -3e38, None, ALU.is_equal).then_inc(mask_ready, 1)

            def softmax(c0, c1):
                dve.wait_ge(ex_done, c1)
                dve.wait_ge(mask_ready, c1)
                exs, total = ex[:, c0:c1, :], gsum[:, c0:c1]
                link(v.tensor_tensor(exs, exs, mask[:, c0:c1, :], ALU.mult))
                link(v.tensor_reduce(total, exs, AX.X, ALU.add))
                link(v.reciprocal(total, total))
                link(v.tensor_tensor(exs, exs, total.unsqueeze(2).to_broadcast([128, c1 - c0, E]), ALU.mult))
                for part in range(3, 6):
                    link(v.tensor_copy(feats[:, c0:c1, :, part], exs))
                    if part < 5:
                        link(v.tensor_tensor(exs, exs, feats[:, c0:c1, :, part], ALU.subtract))

            def ex_split_lo(i, s):
                dve.wait_ge(ex_hi, i * NCH + s + 1)
                v.tensor_tensor(split[:, s % NSPLIT, 1, :], raw_slot(i, s), split[:, s % NSPLIT, 0, :].bitcast(F32),
                                ALU.subtract).then_inc(ex_lo, 1)

            link(v.memset(m8x[:, :], 3e38))
            for n in range(4):
                residual(n)
            norm(0)
            norm(1)
            residual(4)
            residual(5)
            h2_out(0)
            norm(2)
            residual(6)
            choose(0)
            h2_out(1)
            ex_split_lo(0, 0)
            residual(7)
            h2_out(2)
            norm(3)
            choose(1)
            choose(2)
            h2_out(3)
            softmax(0, 3)
            choose(3)
            dve.wait_ge(pos_ps, 1)
            link(v.scalar_tensor_tensor(out=posx[:, :, :], in0=ps[:, 4, 0:128].rearrange("p (c e) -> p c e", e=E),
                                        scalar=1024.0, in1=mask[:, :, :], op0=ALU.add, op1=ALU.mult))
            v.tensor_scalar(posx[:, :, :], posx[:, :, :], -1024.0, None, ALU.add).then_inc(route_ready, 1)
            softmax(3, 4)
            dve.wait_ge(route_ready, 1)

            first = steps[0]

            def serve(i, n_link):
                e, b = i % E, i // E
                v.tensor_scalar(tgt[:, :], posx[:, :, bass.ds(e, 1)].rearrange("p c one -> p (c one)"),
                                passoff[:, bass.ds(b, 1)], None, ALU.subtract).then_inc(dve_step, 1)
                dve.wait_ge(dve_step, n_link)
                v.tensor_tensor(onehot, iota_cap[:, :].unsqueeze(1).to_broadcast([128, NT, CAP]),
                                tgt[:, :].unsqueeze(2).to_broadcast([128, NT, CAP]),
                                ALU.is_equal).then_inc(onehot_ready, 1)

            def index(n, n_link, col):
                dve.wait_ge(idx_done, n)
                v.tensor_copy(f6[:, :], idx_ps).then_inc(dve_step, 1)
                dve.wait_ge(dve_step, n_link)
                v.tensor_reduce(s1[:, :], f6[:, 0:2], AX.X, ALU.add)
                v.tensor_reduce(gates[:, col], f6[:, 3:6], AX.X, ALU.add)
                v.tensor_tensor(s2[:, :], f6[:, 2:3], idle_neg[0:CAP, :], ALU.mult).then_inc(dve_step, 1)
                dve.wait_ge(dve_step, n_link + 1)
                v.scalar_tensor_tensor(out=idx[:, col], in0=s2[:, :], scalar=idle_row[0:CAP, 0:1], in1=s1[:, :],
                                       op0=ALU.add, op1=ALU.add).then_inc(idx_ready, 1)

            def rows_lo(n):
                dve.wait_ge(xt_hi, n)
                for t in range(2):
                    last = v.tensor_tensor(XT[:, 1, 4 * t:4 * t + 4, :],
                                           ps[:, t, 0:4 * CAP].rearrange("p (k n) -> p k n", n=CAP),
                                           XT[:, 0, 4 * t:4 * t + 4, :].bitcast(F32), ALU.subtract)
                last.then_inc(xt_lo, 1)

            def hidden_lo(half, n):
                dve.wait_ge(hidT_hi, n)
                v.tensor_tensor(hidT[:, 1, 4 * half:4 * half + 4, :],
                                ps[:, 6 + half, 0:4 * CAP].rearrange("p (k n) -> p k n", n=CAP),
                                hidT[:, 0, 4 * half:4 * half + 4, :].bitcast(F32),
                                ALU.subtract).then_inc(hidT_lo, 1)

            serve(0, first + 1)
            index(1, first + 2, slice(0, 1))
            serve(1, first + 4)
            dve.wait_ge(idx_ready, 1)
            index(2, first + 5, slice(1, 2))
            steps[0] = first + 6
            link(v.reduce_max(cmax[:, :], ps[:, 4, 128:160], AX.X))
            link(v.tensor_scalar(over[:, 0:PASSES - 1], passoff[:, 1:PASSES], cmax[:, 0:1], None, ALU.is_lt))
            link(v.tensor_reduce(npass[:, :], over[:, 0:PASSES - 1], AX.X, ALU.add))
            link(v.tensor_scalar(npass[:, :], npass[:, :], 1.0, float(E), ALU.add, ALU.mult))
            v.tensor_scalar(items_i[:, 1:2], npass[:, :], -1.0, None, ALU.add)
            v.tensor_copy(items_i[:, 0:1], npass[:, :]).then_inc(items_ready, 1)
            dve.wait_ge(items_ready, 1)
            last_item = dve.value_load(items_i[0:1, 1:2], min_val=E - 1, max_val=E * PASSES - 1)
            base = steps[0] - 3
            for s in range(1, 5):
                ex_split_lo(0, s)
            rows_lo(1)
            ex_split_lo(0, 5)
            PER = 7
            dve.sem_inc(hid_ready, 1)
            dve.sem_inc(hidT_lo, 1)

            def dve_item(i, nxt):
                at = i * PER + base + 3
                dve.wait_ge(idx_done, i + 2)
                serve(i + 2, at + 1)
                e = i % E
                dve.wait_ge(down_begun, i + 1)
                v.tensor_scalar(sel[:, :], part_mod[0:96, :], erow[0:96, bass.ds(e, 1)], None,
                                ALU.is_equal).then_inc(sel_ready, 1)
                ex_split_lo(i, 6)
                dve.wait_ge(y_ready, 2 * i + 1)
                v.tensor_copy(gate_c[:, :], gates[:, bass.ds(i % 4, 1)]).then_inc(gate_ready, 1)
                ex_split_lo(i, 7)
                dve.wait_ge(gate_ready, i + 1)
                dve.wait_ge(idx_ready, i + 2)
                dve.wait_ge(scattered, 16 * i + ADDED - 16)
                index(i + 3, at + 2, bass.ds((i + 2) % 4, 1))
                ex_split_lo(i, 8)
                for half in range(2):
                    b = 2 * half
                    dve.wait_ge(pair_ps, 2 * i + half + 1)
                    dve.wait_ge(hid_ready, 2 * i + half + 1)
                    v.tensor_scalar(gc, ps[0:CAP, b, :], 7.0, None, ALU.min).then_inc(clamp_ready, 1)
                    v.tensor_scalar(uc, ps[0:CAP, b + 1, :], 7.0, -7.0, ALU.min, ALU.max).then_inc(dve_step, 1)
                    dve.wait_ge(dve_step, at + (4 if half == 0 else 6))
                    dve.wait_ge(clamp_ready, 2 * i + half + 1)
                    v.scalar_tensor_tensor(out=uc, in0=uc, scalar=1.0, in1=gc, op0=ALU.add,
                                           op1=ALU.mult).then_inc(dve_step, 1)
                    dve.wait_ge(dve_step, at + (5 if half == 0 else 7))
                    dve.wait_ge(sig_done, 2 * i + half + 1)
                    if half == 0:
                        dve.wait_ge(hidT_ps, 2 * i + 1)
                    v.tensor_tensor(hid[:, half * 512:(half + 1) * 512], uc, sg, ALU.mult).then_inc(hid_ready, 1)
                    if half == 0:
                        ex_split_lo(i, 9)
                        ex_split_lo(i, 10)
                        hidden_lo(0, 2 * i + 1)
                        ex_split_lo(i, 11)
                if nxt:
                    ex_split_lo(i + 1, 0)
                hidden_lo(1, 2 * i + 2)
                if nxt:
                    ex_split_lo(i + 1, 1)
                rows_lo(i + 2)
                if nxt:
                    for s in (2, 3, 4, 5):
                        ex_split_lo(i + 1, s)

            with dve.Fori(0, last_item) as i:
                dve_item(i, True)
            dve_item(last_item, False)

            dve.wait_ge(gfin_in, 16)
            links_done = last_item * PER + PER + base + 3
            for c in range(NT):
                dve.wait_ge(frt_done, c + 1)
                v.reciprocal(rstd[:, c:c + 1], ss[:, c:c + 1]).then_inc(dve_step, 1)
                dve.wait_ge(dve_step, links_done + c + 1)
                v.scalar_tensor_tensor(out=fin[:, c, :], in0=fin[:, c, :], scalar=rstd[:, c:c + 1], in1=gfin,
                                       op0=ALU.mult, op1=ALU.mult).then_inc(out_ready, 1)

        @block.tensor
        def _(pe):
            t_ = nc.tensor
            mm = t_.matmul

            def mm_split(dst, lhsT, rhs, start, stop):
                mm(dst, lhsT(0), rhs(0), start=start, stop=False)
                mm(dst, lhsT(0), rhs(1), start=False, stop=False)
                return mm(dst, lhsT(1), rhs(0), start=False, stop=stop)

            pe.wait_ge(ident_set, 1)
            pe.wait_ge(g_mix_in, 16)
            t_.transpose(ps[:, 7, 0:KD], g16[0:KD, :], ident[0:KD, 0:KD]).then_inc(gcol_ps, 1)
            pe.wait_ge(gcol_ready, 1)
            for c in range(NT):
                pe.wait_ge(xn_ready, c + 1)
                for k in range(KD):
                    last = t_.transpose(ps[:, k, c * 128:(c + 1) * 128], xn[:, c, k * 128:(k + 1) * 128], ident[:, :])
                    if c == NT - 1:
                        last.then_inc(hT_ps, 1)
            for grp in range(7):
                for c in range(4):
                    n = 4 * grp + c
                    if n >= 4:
                        pe.wait_ge(proj_out, n - 3)
                    for k in range(KD):
                        if n == 0:
                            pe.wait_ge(hT_lo, k + 1)
                        elif n < 4 and k == 0:
                            pe.wait_ge(hT_lo, KD)
                        m = 2 * grp + k // 4
                        if c == 0 and k % 4 == 0:
                            pe.wait_ge(in_lo, m + 1)

                        def w(part, lo=0, hi=512):
                            at = (k % 4) * 512
                            return split[:, m % NIN_SPLIT, part, at + lo:at + hi]

                        if grp < 3:
                            last = mm_split(ps[:, n % 4, :], lambda p: hT[:, p, k, c * 128:(c + 1) * 128], w,
                                            start=(k == 0), stop=(k == KD - 1))
                        else:
                            last = mm_split(ps[:, n % 4, :], lambda p: w(p, c * 128, (c + 1) * 128),
                                            lambda p: hT[:, p, k, :], start=(k == 0), stop=(k == KD - 1))
                        if c == 3 and k == 3:
                            last.then_inc(in_used, 1)
                    last.then_inc(proj_ps, 1)
                pe.wait_ge(proj_ps, 4 * grp + 4)
                pe.sem_inc(in_used, 1)
            for n in range(12):
                c, t = n // 3, n % 3
                if t == 0:
                    pe.wait_ge(rope_done, c + 1)
                if n >= 3:
                    pe.wait_ge(qT_a if n % 2 == 0 else qT_d, (n - 3) // 2 + 1)
                for u in range(4):
                    col = (4 * t + u) * 128
                    last = t_.transpose(ps[:, 4 + t, u * 128:(u + 1) * 128], qk[:, c, col:col + 128], ident[:, :])
                last.then_inc(qT_ps, 1)
            pe.wait_ge(qT_a, 6)
            pe.wait_ge(qT_d, 6)
            pe.wait_ge(proj_out, 28)

            pe.wait_ge(pool_consts, 1)
            def scores(j):
                br, h = j // 8, j % 8
                if j:
                    pe.wait_ge(exps_done, 4 * j)
                r = slice(64 * (h % 2), 64 * (h % 2) + 64)
                q, k = qT[r, 6 * br + h // 2, :], qT[r, 6 * br + 4 + h // 4, :]
                for n in range(NT):
                    qn = q[:, n * 128:(n + 1) * 128]
                    if br == 0:
                        last = mm(ps[:, n, :], qn, k, start=True, stop=True)
                        continue
                    w = window(n)
                    c0 = (w[0] - n + 1) * 128
                    mm(ps[:, n, c0:c0 + 128 * len(w)], qn, k[:, w[0] * 128:(w[-1] + 1) * 128], start=True, stop=False)
                    mm(ps[:, n, 0:128], identb[:, :], (mask_lo if n else mask_all)[:, :], start=False, stop=False)
                    last = mm(ps[:, n, 256:384], identb[:, :], (mask_hi if n < NT - 1 else mask_all)[:, :],
                              start=False, stop=True)
                last.then_inc(scores_ps, 1)

            def values(j):
                br, h = j // 8, j % 8
                pe.wait_ge(diag_ready, j + 1)
                for kb in range(NT):
                    m = 4 * j + kb
                    old = m - 3
                    if old >= 0:
                        oj, okb = old // 4, old % 4
                        if okb < 2:
                            pe.wait_ge(pT_a, 2 * oj + okb + 1)
                        else:
                            pe.wait_ge(pT_d, 2 * oj + okb - 1)
                    for n in (range(NT) if br == 0 else window(kb)):
                        c0 = kb * 128 if br == 0 else (kb - n + 1) * 128
                        last = mm(ps[:, 4 + m % 3, n * 128:(n + 1) * 128], probs[:, j % 2, n, c0:c0 + 128],
                                  diag[:, n, :], start=True, stop=True)
                    last.then_inc(pT_ps, 1)
                vc = br * 128 + (h // 4) * 64
                o = ps[64 * (h % 2):64 * (h % 2) + 64, 7, :]
                if h % 2 == 0 and j:
                    pe.wait_ge(oT_out, j // 2)
                if br == 0:
                    for kb in range(NT):
                        if kb < 2:
                            pe.wait_ge(pT_a, 2 * j + kb + 1)
                        else:
                            pe.wait_ge(pT_d, 2 * j + kb - 1)
                        last = mm(o, v_sb[:, kb, vc:vc + 64], pT[:, kb, :], start=(kb == 0), stop=(kb == NT - 1))
                else:
                    pe.wait_ge(pT_a, 2 * j + 2)
                    for n in range(NT):
                        pe.wait_ge(pT_d, 2 * j + (1 if n < 2 else 2))
                        w = window(n)
                        for kb in w:
                            last = mm(o[:, n * 128:(n + 1) * 128], v_sb[:, kb, vc:vc + 64],
                                      pT[:, kb, n * 128:(n + 1) * 128], start=(kb == w[0]), stop=(kb == w[-1]))
                last.then_inc(pv_ps, 1)

            scores(0)
            for j in range(JOBS):
                if j + 1 < JOBS:
                    scores(j + 1)
                values(j)

            pe.wait_ge(oT_lo, 1)
            for c in range(KD):
                pe.wait_ge(br_lo_done, 2 if c < KD // 2 else 4)
                if c >= 2:
                    pe.wait_ge(merged, c - 1)
                for br in range(2):
                    if c == 0 and br:
                        pe.wait_ge(oT_lo, 5)
                    slot = (IN_CHUNKS + 2 * (c // 4) + br) % NIN
                    for k in range(4):
                        at = k * 512 + (c % 4) * 128
                        last = mm_split(ps[:, (c % 2) * 2 + br, :],
                                        lambda p: (br_hi, br_lo)[p][:, slot, at:at + 128],
                                        lambda p: ((oTa_hi, oTa_lo), (oTb_hi, oTb_lo))[br][p][:, k, :],
                                        start=(k == 0), stop=(k == 3))
                last.then_inc(branch_ps, 1)
            pe.wait_ge(branch_ps, KD)
            pe.sem_inc(branches_used, 1)
            pe.sem_inc(ex_used, 1)

            def out_part(n, j):
                c, t = n // 2, n % 2
                if j == 0 and n >= 4:
                    pe.wait_ge(x1_ready, n - 3)
                for k in (2 * j, 2 * j + 1):
                    pe.wait_ge(mT_lo_done, k + 1)
                    at = (k % 2) * D + t * 512
                    last = mm_split(ps[:, 4 + n % 4, :], lambda p: (mT_hi, mT_lo)[p][:, k, c * 128:(c + 1) * 128],
                                    lambda p: (wo_hi, wo_lo)[p][j][:, at:at + 512],
                                    start=(k == 0), stop=(k == KD - 1))
                if j == 3:
                    last.then_inc(wout_ps, 1)

            def out_half(n):
                for j in range(4):
                    out_part(n, j)

            def h2_transpose(c):
                pe.wait_ge(xn2_ready, c + 1)
                if c:
                    pe.wait_ge(h2T_a, c)
                    pe.wait_ge(h2T_d, c)
                for k in range(KD):
                    last = t_.transpose(ps[:, k // 4, (k % 4) * 128:(k % 4 + 1) * 128],
                                        xn2[c][:, k * 128:(k + 1) * 128], ident[:, :])
                last.then_inc(h2T_ps, 1)

            def router(c):
                pe.wait_ge(h2T_a, c + 1)
                pe.wait_ge(h2T_d, c + 1)
                if c >= 2:
                    pe.wait_ge(lg_ready, c - 1)
                for k in range(KD):
                    last = mm(ps[:, 2 + c % 2, c * E:(c + 1) * E], h2T[:, c % 2, k, :], wr[:, k, :],
                              start=(k == 0), stop=(k == KD - 1))
                last.then_inc(logits_ps, 1)

            for j in range(4):
                pe.wait_ge(wo_lo_done, j + 1)
                for n in range(4):
                    out_part(n, j)
            out_half(4)
            out_half(5)
            h2_transpose(0)
            out_half(6)
            router(0)
            h2_transpose(1)
            out_half(7)
            pe.wait_ge(wout_ps, 2 * NT)
            pe.sem_inc(ex_used, NSPLIT - 1)
            h2_transpose(2)
            router(1)
            router(2)
            h2_transpose(3)
            router(3)
            for c in range(NT):
                pe.wait_ge(mask_ready, c + 1)
                for d in range(c + 1):
                    mm(ps[:, 4, c * E:(c + 1) * E], (tri if d == c else onesb)[:, :], mask[:, d, :],
                       start=(d == 0), stop=(d == c))
            for d in range(NT):
                last = mm(ps[:, 4, 128:128 + E], onesb[:, :], mask[:, d, :], start=(d == 0), stop=(d == NT - 1))
            last.then_inc(pos_ps, 1)

            def slots(i, n):
                pe.wait_ge(onehot_ready, n)
                pe.wait_ge(hidT_lo, 2 * i - 3)
                for c in range(NT):
                    last = mm(idx_ps, onehot[:, c, :],
                              feats[:, c, bass.ds(i % E, 1), :].rearrange("p one f -> p (one f)"),
                              start=(c == 0), stop=(c == NT - 1))
                last.then_inc(idx_done, 1)

            def rows_in(n):
                pe.wait_ge(gathered, n * 16)
                for k in range(KD):
                    last = t_.transpose(ps[:, k // 4, (k % 4) * CAP:(k % 4 + 1) * CAP],
                                        xg[:, (k // 2) * 256 + k % 2:(k // 2 + 1) * 256:2], ident[0:CAP, 0:CAP])
                last.then_inc(xt_ps, 1)

            pe.wait_ge(onehot_ready, 1)
            for c in range(NT):
                last = mm(idx_ps, onehot[:, c, :], feats[:, c, 0, :], start=(c == 0), stop=(c == NT - 1))
            last.then_inc(idx_done, 1)
            pe.wait_ge(onehot_ready, 2)
            pe.wait_ge(idx_ready, 1)
            for c in range(NT):
                last = mm(idx_ps, onehot[:, c, :], feats[:, c, 1, :], start=(c == 0), stop=(c == NT - 1))
            last.then_inc(idx_done, 1)
            pe.wait_ge(items_ready, 1)
            items = pe.value_load(items_i[0:1, 0:1], min_val=E, max_val=E * PASSES)
            rows_in(1)
            pe.wait_ge(bias_back, 16)
            pe.sem_inc(down_begun, 1)
            pe.sem_inc(hidT_ps, 1)
            with pe.Fori(0, items) as i:
                def hidden_T(half):
                    pe.wait_ge(hid_ready, 2 * i + half + 2)
                    if half:
                        pe.wait_ge(idx_ready, i + 3)
                    for k in range(4):
                        last = t_.transpose(ps[:, 6 + half, k * CAP:(k + 1) * CAP],
                                            hid[:, half * 512 + (k // 2) * 256 + k % 2:
                                                half * 512 + (k // 2 + 1) * 256:2],
                                            ident[0:CAP, 0:CAP])
                    last.then_inc(hidT_ps, 1)

                pe.wait_ge(xt_lo, i + 1)
                for half in range(2):
                    b = 2 * half
                    if half:
                        pe.wait_ge(hid_ready, 2 * i + 1)
                    for s in range(4 * half, 4 * half + 4):
                        pe.wait_ge(ex_lo, i * NCH + s + 1)
                        for k in range(2):
                            for t in range(2):
                                last = mm_split(ps[0:CAP, b + t, :], lambda p: XT[:, p, 2 * (s % 4) + k, :],
                                                lambda p: expert_w(s, p, k, t),
                                                start=(s % 4 == 0 and k == 0), stop=False)
                        last.then_inc(ex_used, 1)
                        if s == 2:
                            slots(i + 2, i + 3)
                        if s == 6:
                            hidden_T(0)
                    pe.wait_ge(sel_ready, i + 1)
                    for t in range(2):
                        col = t * FF + half * 512
                        last = mm(ps[0:CAP, b + t, :], sel[:, :], bias_tab[0:96, col:col + 512], start=False, stop=True)
                    last.then_inc(pair_ps, 1)

                pe.wait_ge(y_ready, 2 * i + 1)
                for t in range(2):
                    col = 2 * FF + t * 512
                    last = mm(ps[0:CAP, 4 + t, :], sel[:, :], bias_tab[0:96, col:col + 512], start=True, stop=False)
                last.then_inc(down_begun, 1)
                for half in range(2):
                    if half:
                        hidden_T(1)
                        rows_in(i + 2)
                    pe.wait_ge(hidT_lo, 2 * i + half + 2)
                    for s in range(8 + 2 * half, 10 + 2 * half):
                        pe.wait_ge(ex_lo, i * NCH + s + 1)
                        for k in range(2):
                            for t in range(2):
                                last = mm_split(ps[0:CAP, 4 + t, :], lambda p: hidT[:, p, 2 * (s - 8) + k, :],
                                                lambda p: expert_w(s, p, k, t),
                                                start=False, stop=(s == 11 and k == 1))
                        last.then_inc(ex_used, 1)


_INS = ['x', 'g_mix', 'w_in', 'qa_norm', 'ka_norm', 'sink_b', 'w_branch_a', 'w_branch_b', 'w_out', 'g_ffn', 'w_router',
        'b_router', 'w_gate_up', 'b_gate_up', 'w_down', 'b_down', 'g_final']


def rope_tables():
    grid = 64
    t = np.arange(SEQ)
    inv_ax = np.float32(10000.0) ** (-np.arange(0, HD // 2, 2, dtype=np.float32) / np.float32(HD // 2))
    inv_1d = np.float32(10000.0) ** (-np.arange(0, HD, 2, dtype=np.float32) / np.float32(HD))
    row, col = (t // grid).astype(np.float32), (t % grid).astype(np.float32)
    ax = np.concatenate([row[:, None] * inv_ax, col[:, None] * inv_ax], axis=-1).astype(np.float32)
    d1 = (t.astype(np.float32)[:, None] * inv_1d).astype(np.float32)
    return np.stack([np.cos(ax), np.sin(ax), np.cos(d1), np.sin(d1)], axis=1).astype(np.float32)


def kernel(**inputs):
    import concourse.bacc as _bacc
    from concourse.bass_utils import run_bass_kernel_spmd as _run

    nc = _bacc.Bacc("TRN2", target_bir_lowering=False, num_devices=1)
    f32 = mybir.dt.float32
    arrays, args = {}, []
    for name in _INS:
        a = np.ascontiguousarray(inputs[name])
        arrays[f"in_{name}"] = a
        args.append(nc.dram_tensor(f"in_{name}", a.shape, mybir.dt.from_np(a.dtype), kind="ExternalInput").ap())
    tables = rope_tables()
    arrays["rope_tables"] = tables
    args.append(nc.dram_tensor("rope_tables", tables.shape, f32, kind="ExternalInput").ap())
    args.append(nc.dram_tensor("h2_rows", (SEQ + CAP, D), f32, kind="Internal").ap())
    args.append(nc.dram_tensor("sum_rows", (SEQ + CAP, D), f32, kind="Internal").ap())
    args.append(nc.dram_tensor("bias_parts", (E * 3, 3 * D), mybir.dt.bfloat16, kind="Internal").ap())
    args.append(nc.dram_tensor("out", (1, SEQ, D), f32, kind="ExternalOutput").ap())
    encoder_block(nc, *args)
    r = _run(nc, [arrays], core_ids=[0])
    return r.results[0]["out"]
```
